# Optimizing a Trainium2 kernel written in Bass

```python
import math
import jax
import jax.numpy as jnp
from jax import lax
import numpy as np

D_MODEL = 1024
BATCH = 1
SEQ = 4096
DEPTH = 1
DEC_BATCH = 8
DEC_SEQ = 16
PAST_LEN = 1024

CHUNK = 64
PLE_DIM = 256
H_A = 8
DK = 64
DV = 64
W_A = H_A * DV
QKV_A = 2 * H_A * DK + H_A * DV
CONV_W = 4
H_B = 8
D_B = 64
W_B = H_B * D_B
LEFT_CHUNKS = 8
BAND_PAST = LEFT_CHUNKS * CHUNK
MAX_REL = 128
N_REL = 2 * MAX_REL + 1
D_MIX = W_A + W_B
SPLIT_SIZES = (QKV_A, H_A, H_A, W_A, W_B, W_B, W_B, W_B)
D_PROJ = sum(SPLIT_SIZES)
EPS = 1e-6

kernel_name = 'hybrid_gdn_chunkband_streaming_step'

def rms_norm(x, g):
    xf = x.astype(jnp.float32)
    y = xf * lax.rsqrt(jnp.mean(xf * xf, axis=-1, keepdims=True) + EPS)
    return (y * g.astype(jnp.float32)).astype(x.dtype)

def l2_norm(x):
    xf = x.astype(jnp.float32)
    return (xf * lax.rsqrt(jnp.sum(xf * xf, axis=-1, keepdims=True) + EPS)).astype(x.dtype)

def _gated_delta_blocked(q, k, v, g, beta, s0):
    b, t, h, _ = q.shape
    dv = v.shape[-1]
    out_dtype, st_dtype = v.dtype, s0.dtype
    blen = min(CHUNK, t)
    n = t // blen
    f32 = jnp.float32

    def blk(a):
        return a.astype(f32).reshape(b, n, blen, h, -1).transpose(0, 3, 1, 2, 4)

    q, k, v = blk(q), blk(k), blk(v)
    g = g.astype(f32).reshape(b, n, blen, h).transpose(0, 3, 1, 2)
    beta = beta.astype(f32).reshape(b, n, blen, h).transpose(0, 3, 1, 2)
    gc = jnp.cumsum(g, axis=-1)
    incl = jnp.tril(jnp.ones((blen, blen), bool))
    strict = jnp.tril(jnp.ones((blen, blen), bool), -1)
    decay = jnp.exp(jnp.where(incl, gc[..., :, None] - gc[..., None, :], -jnp.inf))
    kk = jnp.einsum('bhnid,bhnjd->bhnij', k, k)
    lower = jnp.where(strict, beta[..., :, None] * kk * decay, 0.0) + jnp.eye(blen, dtype=f32)
    rhs = jnp.concatenate([v * beta[..., None], k * (beta * jnp.exp(gc))[..., None]], axis=-1)
    sol = lax.linalg.triangular_solve(lower, rhs, left_side=True, lower=True)
    u, w = sol[..., :dv], sol[..., dv:]
    qk = jnp.einsum('bhnid,bhnjd->bhnij', q, k) * decay
    q_dec = q * jnp.exp(gc)[..., None]
    k_tail = k * jnp.exp(gc[..., -1:] - gc)[..., None]
    g_tot = jnp.exp(gc[..., -1])

    def step(s, xs):
        u_c, w_c, qk_c, qd_c, kt_c, gt_c = xs
        v_new = u_c - jnp.einsum('bhld,bhde->bhle', w_c, s)
        o_c = jnp.einsum('bhld,bhde->bhle', qd_c, s) + jnp.einsum('bhij,bhje->bhie', qk_c, v_new)
        s = s * gt_c[..., None, None] + jnp.einsum('bhld,bhle->bhde', kt_c, v_new)
        return s, o_c

    xs = tuple(jnp.moveaxis(a, 2, 0) for a in (u, w, qk, q_dec, k_tail, g_tot))
    s_fin, o = lax.scan(step, s0.astype(f32), xs)
    o = o.transpose(1, 0, 3, 2, 4).reshape(b, t, h, dv)
    return o.astype(out_dtype), s_fin.astype(st_dtype)

def _rel_bias(table, qpos, kpos):
    rel = jnp.clip(qpos[:, None] - kpos[None, :], -MAX_REL, MAX_REL) + MAX_REL
    return table[:, rel].astype(jnp.float32)

def _softmax_attend(q, k, v, bias, valid=None):
    s = jnp.einsum('bqhd,bkhd->bhqk', q, k).astype(jnp.float32) * (D_B ** -0.5) + bias
    if valid is not None:
        s = jnp.where(valid, s, -jnp.inf)
    p = jax.nn.softmax(s, axis=-1)
    return jnp.einsum('bhqk,bkhd->bqhd', p.astype(v.dtype), v)

def _band_attention_prompt(q, k, v, table):
    b, t, h, d = q.shape
    n = t // CHUNK
    span = BAND_PAST + CHUNK
    kpad = jnp.pad(k, ((0, 0), (BAND_PAST, 0), (0, 0), (0, 0)))
    vpad = jnp.pad(v, ((0, 0), (BAND_PAST, 0), (0, 0), (0, 0)))
    bias = _rel_bias(table, BAND_PAST + jnp.arange(CHUNK), jnp.arange(span))
    qc = jnp.moveaxis(q.reshape(b, n, CHUNK, h, d), 1, 0)

    def one(args):
        c, qb = args
        start = c * CHUNK
        kb = lax.dynamic_slice_in_dim(kpad, start, span, axis=1)
        vb = lax.dynamic_slice_in_dim(vpad, start, span, axis=1)
        valid = (start + jnp.arange(span)) >= BAND_PAST
        return _softmax_attend(qb, kb, vb, bias, valid)

    o = lax.map(one, (jnp.arange(n), qc))
    return jnp.moveaxis(o, 0, 1).reshape(b, t, h, d)

def _band_attention_sample(q, k_new, v_new, k_cache, v_cache, table):
    wc = k_cache.shape[1]
    tn = q.shape[1]
    kb = jnp.concatenate([k_cache, k_new], axis=1)
    vb = jnp.concatenate([v_cache, v_new], axis=1)
    bias = _rel_bias(table, wc + jnp.arange(tn), jnp.arange(wc + tn))
    return _softmax_attend(q, kb, vb, bias)

def _layer(h, p_i, conv0, s0, k_cache, v_cache, ln_g, w_in, conv_w, a_log, dt_bias,
           gdn_norm_g, q_norm_g, k_norm_g, rel_bias, w_out, w_ple_proj, ple_norm_g, w_ple_gate):
    b, t, _ = h.shape
    xn = rms_norm(h, ln_g)
    proj = xn @ w_in
    split_at = np.cumsum(SPLIT_SIZES)[:-1].tolist()
    qkv_a, a_raw, b_raw, z_a, q_b, k_b, v_b, z_b = jnp.split(proj, split_at, axis=-1)

    xcat = jnp.concatenate([conv0, qkv_a], axis=1)
    conv = sum(xcat[:, j:j + t] * conv_w[j] for j in range(CONV_W))
    new_conv = xcat[:, xcat.shape[1] - (CONV_W - 1):]
    conv = jax.nn.silu(conv)
    q_a, k_a, v_a = jnp.split(conv, [H_A * DK, 2 * H_A * DK], axis=-1)
    q_a = l2_norm(q_a.reshape(b, t, H_A, DK)) * (DK ** -0.5)
    k_a = l2_norm(k_a.reshape(b, t, H_A, DK))
    v_a = v_a.reshape(b, t, H_A, DV)
    beta = jax.nn.sigmoid(b_raw.astype(jnp.float32))
    g = -jnp.exp(a_log.astype(jnp.float32)) * jax.nn.softplus(
        a_raw.astype(jnp.float32) + dt_bias.astype(jnp.float32))
    o_a, s_new = _gated_delta_blocked(q_a, k_a, v_a, g, beta, s0)
    o_a = rms_norm(o_a, gdn_norm_g).reshape(b, t, W_A) * jax.nn.silu(z_a)

    q_b = rms_norm(q_b.reshape(b, t, H_B, D_B), q_norm_g)
    k_b = rms_norm(k_b.reshape(b, t, H_B, D_B), k_norm_g)
    v_b = v_b.reshape(b, t, H_B, D_B)
    if k_cache is None:
        o_b = _band_attention_prompt(q_b, k_b, v_b, rel_bias)
        keep = min(BAND_PAST, t)
        k_state, v_state = k_b[:, t - keep:], v_b[:, t - keep:]
    else:
        o_b = _band_attention_sample(q_b, k_b, v_b, k_cache, v_cache, rel_bias)
        k_state, v_state = k_b, v_b
    o_b = o_b.reshape(b, t, W_B) * jax.nn.silu(z_b)

    h = h + jnp.concatenate([o_a, o_b], axis=-1) @ w_out
    e = rms_norm(p_i @ w_ple_proj, ple_norm_g)
    h = h + jax.nn.sigmoid(h @ w_ple_gate) * e
    return h, new_conv, s_new, k_state, v_state

def setup_inputs(seed: int = 0) -> dict:
    key = jax.random.key(seed)
    ks = jax.random.split(key, 24)
    f32 = jnp.float32

    def nrm(k, shape, s):
        return jax.random.normal(k, shape, f32) * s

    wc = min(BAND_PAST, PAST_LEN)
    dt = jnp.exp(jax.random.uniform(ks[12], (DEPTH, H_A), f32, math.log(1e-3), math.log(1e-1)))
    return {
        'x_prompt': nrm(ks[0], (BATCH, SEQ, D_MODEL), 1.0),
        'x_sample': nrm(ks[1], (DEC_BATCH, DEC_SEQ, D_MODEL), 1.0),
        'state_conv': nrm(ks[2], (DEPTH, DEC_BATCH, CONV_W - 1, QKV_A), 1.0),
        'state_gdn': nrm(ks[3], (DEPTH, DEC_BATCH, H_A, DK, DV), 0.3),
        'cache_k': nrm(ks[4], (DEPTH, DEC_BATCH, wc, H_B, D_B), 1.0),
        'cache_v': nrm(ks[5], (DEPTH, DEC_BATCH, wc, H_B, D_B), 1.0),
        'p_prompt': nrm(ks[6], (DEPTH, BATCH, SEQ, PLE_DIM), 1.0),
        'p_sample': nrm(ks[7], (DEPTH, DEC_BATCH, DEC_SEQ, PLE_DIM), 1.0),
        'ln_g': 1.0 + nrm(ks[8], (DEPTH, D_MODEL), 0.05),
        'w_in': nrm(ks[9], (DEPTH, D_MODEL, D_PROJ), D_MODEL ** -0.5),
        'conv_w': nrm(ks[10], (DEPTH, CONV_W, QKV_A), CONV_W ** -0.5),
        'a_log': jnp.log(jax.random.uniform(ks[11], (DEPTH, H_A), f32, 1.0, 16.0)),
        'dt_bias': dt + jnp.log(-jnp.expm1(-dt)),
        'gdn_norm_g': 1.0 + nrm(ks[13], (DEPTH, DV), 0.05),
        'q_norm_g': 1.0 + nrm(ks[14], (DEPTH, D_B), 0.05),
        'k_norm_g': 1.0 + nrm(ks[15], (DEPTH, D_B), 0.05),
        'rel_bias': nrm(ks[16], (DEPTH, H_B, N_REL), 0.5),
        'w_out': nrm(ks[17], (DEPTH, D_MIX, D_MODEL), D_MIX ** -0.5),
        'w_ple_proj': nrm(ks[18], (DEPTH, PLE_DIM, D_MODEL), PLE_DIM ** -0.5),
        'ple_norm_g': 1.0 + nrm(ks[19], (DEPTH, D_MODEL), 0.05),
        'w_ple_gate': nrm(ks[20], (DEPTH, D_MODEL, D_MODEL), D_MODEL ** -0.5),
    }

def reference(x_prompt, x_sample, state_conv, state_gdn, cache_k, cache_v, p_prompt, p_sample,
              ln_g, w_in, conv_w, a_log, dt_bias, gdn_norm_g, q_norm_g, k_norm_g, rel_bias,
              w_out, w_ple_proj, ple_norm_g, w_ple_gate):
    hp, hs = x_prompt, x_sample
    bp = x_prompt.shape[0]
    conv_p, gdn_p, kp, vp = [], [], [], []
    conv_s, gdn_s, ksm, vsm = [], [], [], []
    for i in range(DEPTH):
        w_i = (ln_g[i], w_in[i], conv_w[i], a_log[i], dt_bias[i], gdn_norm_g[i], q_norm_g[i],
               k_norm_g[i], rel_bias[i], w_out[i], w_ple_proj[i], ple_norm_g[i], w_ple_gate[i])
        conv0 = jnp.zeros((bp, CONV_W - 1, QKV_A), x_prompt.dtype)
        s0 = jnp.zeros((bp, H_A, DK, DV), x_prompt.dtype)
        hp, c_p, g_p, k_p, v_p = _layer(hp, p_prompt[i], conv0, s0, None, None, *w_i)
        hs, c_s, g_s, k_s, v_s = _layer(hs, p_sample[i], state_conv[i], state_gdn[i],
                                        cache_k[i], cache_v[i], *w_i)
        conv_p.append(c_p); gdn_p.append(g_p); kp.append(k_p); vp.append(v_p)
        conv_s.append(c_s); gdn_s.append(g_s); ksm.append(k_s); vsm.append(v_s)
    conv_prompt = jnp.stack(conv_p)
    gdn_prompt = jnp.stack(gdn_p)
    k_prompt = jnp.stack(kp)
    v_prompt = jnp.stack(vp)
    conv_sample = jnp.stack(conv_s)
    gdn_sample = jnp.stack(gdn_s)
    k_sample = jnp.stack(ksm)
    v_sample = jnp.stack(vsm)
    return (hp, hs, conv_prompt, gdn_prompt, k_prompt, v_prompt,
            conv_sample, gdn_sample, k_sample, v_sample)


_drawn_inputs = setup_inputs


def setup_inputs(seed=0):
    import zlib

    import numpy as np

    out = dict(_drawn_inputs(seed))
    spreads = {}
    factors = {'cache_k': 2.782,
     'gdn_norm_g': 3.034,
     'q_norm_g': 8.0,
     'rel_bias': 5.279,
     'ple_norm_g': 3.501}
    for name, (base, spread) in spreads.items():
        noise = np.random.default_rng([zlib.crc32(name.encode()), seed]).standard_normal(out[name].shape)
        drawn = base * np.exp(spread * noise) if base else spread * noise
        out[name] = jnp.asarray(drawn.astype(out[name].dtype))
    for name, factor in factors.items():
        out[name] = (out[name] * factor).astype(out[name].dtype)
    return out
```

```python
from contextlib import ExitStack

import concourse.bass as bass
import numpy as np
from concourse import mybir

F32 = mybir.dt.float32
F32R = mybir.dt.float32r
ACT = mybir.ActivationFunctionType
ALU = mybir.AluOpType
AX = mybir.AxisListType

P = 128
EPS = 1e-6


class Phase:

    def __init__(self, nc, stack):
        self.nc, self.stack, self.sems = nc, stack, []
        stack.callback(self.end)

    def sb(self, name, shape, dt=F32):
        return self.stack.enter_context(self.nc.sbuf_tensor(name, shape, dt))

    def ps(self, name, shape, dt=F32):
        return self.stack.enter_context(self.nc.psum_tensor(name, shape, dt))

    def sem(self, name):
        self.sems.append(self.nc.alloc_semaphore(name=name))
        return self.sems[-1]

    def end(self):
        self.nc.clear_and_free_semaphores(self.sems)
        self.nc.all_engine_barrier()


def waits_apart(eng, met, waits):
    regs = [(sem, value if isinstance(value, int) else eng.to_reg(value)) for sem, value in waits]
    eng.wait_ge(*met)
    for sem, value in regs:
        if not isinstance(value, int) or value > 0:
            eng.wait_ge(sem, value)


def after_none(eng, sem, value):
    if not isinstance(value, int) or value > 0:
        eng.wait_ge(sem, value)


def identity(eng, tile, filled):
    eng.memset(tile[:, :], 0.0).then_inc(filled, 1)
    eng.wait_ge(filled, 1)
    eng.affine_select(out=tile[:, :], in_=tile[:, :], compare_op=ALU.not_equal, fill=1.0, base=0,
                      pattern=[[-1, P]], channel_multiplier=1).then_inc(filled, 1)


def matmul3(nc, out, x_hi, x_lo, w_hi, w_lo, first, last):
    nc.tensor.matmul(out, x_hi, w_hi, start=first, stop=False)
    nc.tensor.matmul(out, x_hi, w_lo, start=False, stop=False)
    return nc.tensor.matmul(out, x_lo, w_hi, start=False, stop=last)


def load_weight(sp, k, stages, rows, there, lo_ok):
    if k >= len(stages):
        sp.wait_ge(lo_ok, k - len(stages) + 1)
    sp.dma_start(stages[k % len(stages)], rows).then_inc(there[k], 16)


def weight_hi(e, k, stages, hi, there, hi_ok):
    e.wait_ge(there[k], 16)
    e.activation(hi[k], stages[k % len(stages)], ACT.Copy).then_inc(hi_ok, 1)


def weight_lo(v, k, stages, hi, lo, hi_ok, lo_ok):
    v.wait_ge(hi_ok, k + 1)
    v.tensor_tensor(lo[k], stages[k % len(stages)], hi[k].bitcast(F32), ALU.subtract).then_inc(lo_ok, 1)


def project_a(nc, d, s):
    D, KT, QKV = s.D, s.D // P, s.QKV
    BLOCKS = s.SEQ // (2 * P)
    G = QKV // P
    HA, N, HALO, TAPS = s.HA, 2 * P, s.CONVW - 1, s.CONVW
    WCOLS = QKV + 2 * HA
    with ExitStack() as stack:
        ph = Phase(nc, stack)
        w_hi = ph.sb("a_w_hi", [P, KT, WCOLS], F32R)
        w_lo = ph.sb("a_w_lo", [P, KT, WCOLS], F32R)
        x_raw = [ph.sb(f"a_x{i}", [P, D]) for i in range(2)]
        squares = ph.sb("a_squares", [P, D], mybir.dt.bfloat16)
        x_full = ph.sb("a_x_full", [P, KT, P])
        xT_hi = [ph.sb(f"a_xT_hi{i}", [P, KT, N], F32R) for i in range(2)]
        xT_lo = [ph.sb(f"a_xT_lo{i}", [P, KT, N], F32R) for i in range(2)]
        raw = [ph.sb(f"a_raw{i}", [P, G, HALO + N]) for i in range(2)]
        act = [ph.sb(f"a_act{i}", [P, G, N]) for i in range(2)]
        taps = ph.sb("a_taps", [P, TAPS, G])
        lnT = ph.sb("a_lnT", [P, KT])
        ident = ph.sb("a_ident", [P, P])
        ssq = ph.sb("a_ssq", [P, 2])
        var = ph.sb("a_var", [P, 2])
        rstd = ph.sb("a_rstd", [P, 2])
        neg_half = ph.sb("a_neg_half", [P, 2])
        dt_b = ph.sb("a_dt", [2 * HA, 1])
        alog = ph.sb("a_alog", [2 * HA, 1])
        rate = ph.sb("a_rate", [2 * HA, 1])
        gate = ph.sb("a_gate", [2 * HA, N])
        gate_s = ph.sb("a_gate_s", [2 * HA, N])
        xa, na, u, en, w, ln_w, c, sp_, gc, beta = (ph.sb(f"a_{k}", [2 * HA, N]) for k in (
            "xa", "na", "u", "en", "w", "ln_w", "c", "softplus", "gc", "beta"))
        nx, rx, g_, bden = sp_, c, ln_w, w

        psT = ph.ps("a_psT", [P, KT * P])
        psG = [ph.ps(f"a_psG{i}", [P, 512]) for i in range(4)]
        psAB = ph.ps("a_psAB", [P, 512])

        consts = ph.sem("a_consts")
        filled = ph.sem("a_filled")
        cleared = ph.sem("a_cleared")
        rated = ph.sem("a_rated")
        w_in = [ph.sem(f"a_w_in{k}") for k in range(KT)]
        w_hi_ok = ph.sem("a_w_hi_ok")
        w_lo_ok = ph.sem("a_w_lo_ok")
        x_in = [ph.sem(f"a_x_in{i}") for i in range(2)]
        ssq_ok = ph.sem("a_ssq_ok")
        var_ok = ph.sem("a_var_ok")
        rstd_ok = ph.sem("a_rstd_ok")
        scaled = ph.sem("a_scaled")
        xT_ps = ph.sem("a_xT_ps")
        full_ok = ph.sem("a_full_ok")
        hi_ok = ph.sem("a_hi_ok")
        lo_ok = ph.sem("a_lo_ok")
        grp_ok = ph.sem("a_grp_ok")
        evac = ph.sem("a_evac")
        halo_ok = ph.sem("a_halo_ok")
        conv = ph.sem("a_conv")
        silu = ph.sem("a_silu")
        ab_ok = ph.sem("a_ab_ok")
        ab_v = ph.sem("a_ab_v")
        ab_s = ph.sem("a_ab_s")
        stored = [ph.sem(f"a_stored{i}") for i in range(2)]
        ab_stored = ph.sem("a_ab_stored")
        last_rows = ph.sem("a_last_rows")
        V_AB, S_AB = 11, 3

        flat = [x[i][:, :, :].rearrange("p g n -> p (g n)") for x in (raw, act) for i in range(2)]
        parts_hi, parts_lo = ([w[:, k, :] for k in range(KT)] for w in (w_hi, w_lo))
        stages = [x[:, 0:WCOLS] for x in flat] + [x[:, WCOLS:2 * WCOLS] for x in flat[0:2]]
        block = stack.enter_context(nc.Block())

        @block.sync
        def _(sp):
            with nc.allow_non_contiguous_dma(reason="small per-channel constants, once"):
                sp.dma_start(lnT[:, :], d.ln_g.rearrange("(k p) -> p k", p=P)).then_inc(consts, 16)
                for j in range(TAPS):
                    sp.dma_start(taps[:, j, :], d.conv_w[j, :].rearrange("(g p) -> p g", p=P)).then_inc(consts, 16)
                sp.wait_ge(cleared, 2)
                sp.dma_start(dt_b[0:HA, :], d.dt_bias.rearrange("(h o) -> h o", o=1)).then_inc(consts, 16)
                sp.dma_start(alog[0:HA, :], d.a_log.rearrange("(h o) -> h o", o=1)).then_inc(consts, 16)
            for a in range(2):
                sp.dma_start(x_raw[a][:, :], d.x_p[a * P:(a + 1) * P, :]).then_inc(x_in[a], 16)
            for k in range(KT):
                load_weight(sp, k, stages, d.w_in[k * P:(k + 1) * P, 0:WCOLS], w_in, w_lo_ok)
            for a in range(2):
                sp.wait_ge(xT_ps, a + 1)
                sp.dma_start(x_raw[a][:, :], d.x_p[N + a * P:N + (a + 1) * P, :]).then_inc(x_in[a], 16)

            def load_ahead(b, src):
                for a in range(2):
                    sp.wait_ge(xT_ps, 2 * b + a + 3)
                    sp.dma_start(x_raw[a][:, :], src(a)).then_inc(x_in[a], 16)

            def store_ab(b, n):
                sp.wait_ge(ab_v, V_AB * (b + 1))
                sp.dma_start(d.gcT[:, bass.ds(b * N, n)], gc[0:HA, 0:n]).then_inc(ab_stored, 16)
                sp.dma_start(d.betaT[:, bass.ds(b * N, n)], beta[HA:2 * HA, 0:n]).then_inc(ab_stored, 16)

            def store(b, par):
                sp.wait_ge(silu, G * (b + 1))
                sp.dma_start(d.qkvT[:, bass.ds(b * N, N)].rearrange("(g p) t -> p g t", p=P),
                             act[par][:, :, :]).then_inc(stored[par], 16)
                store_ab(b, N)

            with sp.Fori(0, BLOCKS // 2 - 1) as i:
                for par in range(2):
                    b = 2 * i + par
                    load_ahead(b, lambda a: d.x_p[bass.ds((b + 2) * N + a * P, P), :])
                    store(b, par)
            load_ahead(BLOCKS - 2, lambda a: d.x_s)
            store(BLOCKS - 2, 0)
            with nc.allow_non_contiguous_dma(reason="three columns, once"):
                sp.wait_ge(evac, 4 + G * BLOCKS)
                sp.dma_start(d.lastT.rearrange("(g p) t -> p g t", p=P), raw[1][:, :, N:]).then_inc(last_rows, 16)
            store(BLOCKS - 1, 1)
            sp.wait_ge(evac, 4 + G * (BLOCKS + 1))
            sp.dma_start(d.rawT_s.rearrange("(g p) t -> p g t", p=P), raw[0][:, :, HALO:HALO + P]).then_inc(last_rows, 16)
            store_ab(BLOCKS, P)
            for par in range(2):
                sp.wait_ge(stored[par], 16 * (1 + BLOCKS // 2))
            sp.wait_ge(ab_stored, 32 * (BLOCKS + 2))
            sp.wait_ge(last_rows, 32)

        @block.gpsimd
        def _(pool):
            identity(pool, ident, filled)
            pool.memset(neg_half[:, :], -0.5).then_inc(filled, 1)
            pool.wait_ge(filled, 3)

            def norm(t, a):
                waits_apart(pool, (filled, 3), [(ssq_ok, t + 1)])
                pool.tensor_scalar(var[:, a:a + 1], ssq[:, a:a + 1], 1.0 / D, EPS, ALU.mult, ALU.add).then_inc(var_ok, 1)
                pool.wait_ge(var_ok, t + 1)
                pool.tensor_tensor(rstd[:, a:a + 1], var[:, a:a + 1], neg_half[:, a:a + 1], ALU.pow).then_inc(rstd_ok, 1)

            for a in range(2):
                norm(a, a)
            with pool.Fori(0, BLOCKS) as b:
                for a in range(2):
                    norm(2 * b + 2 + a, a)

        @block.scalar
        def _(e):
            e.sem_inc(evac, 4)
            e.wait_ge(consts, 16 * (TAPS + 3))
            e.activation(rate[:, :], alog[:, :], ACT.Exp).then_inc(rated, 1)

            def square(t, b, a, first=False):
                e.wait_ge(x_in[a], 16 * (b + 1))
                if not first:
                    e.wait_ge(ssq_ok, t)
                e.activation(squares[:, :], x_raw[a][:, :], ACT.Square, accum_out=ssq[:, a:a + 1]).then_inc(ssq_ok, 1)

            def scale(t, a):
                e.wait_ge(rstd_ok, t + 1)
                e.activation(x_raw[a][:, :], x_raw[a][:, :], ACT.Copy, scale=rstd[:, a:a + 1]).then_inc(scaled, 1)

            def split_hi(t, par, a):
                e.wait_ge(full_ok, t + 1)
                e.activation(xT_hi[par][:, :, a * P:(a + 1) * P], x_full[:, :, :], ACT.Copy).then_inc(hi_ok, 1)

            square(0, 0, 0, first=True)
            square(1, 0, 1)
            scale(0, 0)
            scale(1, 1)
            for k in range(KT):
                weight_hi(e, k, stages, parts_hi, w_in, w_hi_ok)
                if k == 3:
                    split_hi(0, 0, 0)
                if k == 5:
                    split_hi(1, 0, 1)

            def run_block(b, par, tail=False):
                def conv_silu(g):
                    e.wait_ge(conv, TAPS * (G * b + g + 1))
                    e.activation(act[par][:, g, :], act[par][:, g, :], ACT.Silu).then_inc(silu, 1)

                for g in range(G):
                    e.wait_ge(grp_ok, G * b + g + 1)
                    if g == 0:
                        e.wait_ge(halo_ok, b + 1)
                    e.activation(raw[par][:, g, HALO:], psG[g % 4][:, 0:N], ACT.Copy).then_inc(evac, 1)
                    if not tail:
                        if g == 0:
                            square(2 * b + 2, b + 1, 0)
                        if g == 1:
                            scale(2 * b + 2, 0)
                        if g >= 1:
                            conv_silu(g - 1)
                        if g == 4:
                            split_hi(2 * b + 2, 1 - par, 0)
                        if g == 5:
                            square(2 * b + 3, b + 1, 1)
                        if g == 6:
                            scale(2 * b + 3, 1)
                        if g == 9:
                            split_hi(2 * b + 3, 1 - par, 1)
                if not tail:
                    conv_silu(G - 1)
                    e.wait_ge(evac, 4 + G * (b + 1))
                    e.activation(raw[1 - par][:, :, 0:HALO], raw[par][:, :, N:], ACT.Copy).then_inc(halo_ok, 1)
                e.wait_ge(ab_v, V_AB * b + 3)
                e.activation(u[:, :], na[:, :], ACT.Exp).then_inc(ab_s, 1)
                e.activation(en[:, :], xa[:, :], ACT.Exp, scale=-1.0).then_inc(ab_s, 1)
                e.wait_ge(ab_v, V_AB * b + 4)
                e.activation(ln_w[:, :], w[:, :], ACT.Ln).then_inc(ab_s, 1)

            with e.Fori(0, BLOCKS // 2) as i:
                for par in range(2):
                    run_block(2 * i + par, par)
            run_block(BLOCKS, 0, tail=True)

        @block.tensor
        def _(pe):
            pe.wait_ge(filled, 2)

            def transposes(t, a):
                pe.wait_ge(scaled, t + 1)
                after_none(pe, full_ok, t)
                for k in range(KT):
                    last = nc.tensor.transpose(psT[:, k * P:(k + 1) * P], x_raw[a][:, k * P:(k + 1) * P], ident[:, :])
                last.then_inc(xT_ps, 1)

            transposes(0, 0)
            transposes(1, 1)
            pe.wait_ge(w_lo_ok, KT)

            def product(out, cols, par):
                for k in range(KT):
                    last = matmul3(nc, out, w_hi[:, k, cols], w_lo[:, k, cols], xT_hi[par][:, k, :],
                                   xT_lo[par][:, k, :], k == 0, k == KT - 1)
                return last

            def run_block(b, par, tail=False):
                pe.wait_ge(lo_ok, 2 * (b + 1))
                for g in range(G):
                    pe.wait_ge(evac, G * b + g + 1)
                    product(psG[g % 4][:, 0:N], slice(g * P, (g + 1) * P), par).then_inc(grp_ok, 1)
                    if g == 3 and not tail:
                        transposes(2 * b + 2, 0)
                    if g == 8 and not tail:
                        transposes(2 * b + 3, 1)
                product(psAB[0:2 * HA, 0:N], slice(QKV, WCOLS), par).then_inc(ab_ok, 1)

            with pe.Fori(0, BLOCKS // 2) as i:
                for par in range(2):
                    run_block(2 * i + par, par)
            run_block(BLOCKS, 0, tail=True)

        @block.vector
        def _(v):
            v.memset(dt_b[:, :], 0.0).then_inc(cleared, 1)
            v.memset(alog[:, :], 0.0).then_inc(cleared, 1)
            v.memset(gate[:, :], 1.0).then_inc(cleared, 1)
            v.memset(gate_s[:, :], 1.0).then_inc(cleared, 1)
            v.wait_ge(cleared, 4)
            v.memset(gate[:, 0:N:P], 0.0).then_inc(cleared, 1)
            v.memset(gate_s[:, 0:N:s.DECT], 0.0).then_inc(cleared, 1)
            v.sem_inc(stored[0], 16)
            v.sem_inc(stored[1], 16)
            v.sem_inc(ab_stored, 32)
            v.wait_ge(consts, 16 * (TAPS + 3))

            def full(t, first=False):
                v.wait_ge(xT_ps, t + 1)
                if not first:
                    v.wait_ge(lo_ok, t)
                v.tensor_tensor(x_full[:, :, :], psT[:, :].rearrange("p (k n) -> p k n", k=KT),
                                lnT[:, :].unsqueeze(2).to_broadcast([P, KT, P]), ALU.mult).then_inc(full_ok, 1)

            def split_lo(t, par, a):
                v.wait_ge(hi_ok, t + 1)
                v.tensor_tensor(xT_lo[par][:, :, a * P:(a + 1) * P], x_full[:, :, :],
                                xT_hi[par][:, :, a * P:(a + 1) * P].bitcast(F32), ALU.subtract).then_inc(lo_ok, 1)

            for k in range(KT):
                weight_lo(v, k, stages, parts_hi, parts_lo, w_hi_ok, w_lo_ok)
                if k == 2:
                    full(0, first=True)
                if k == 3:
                    split_lo(0, 0, 0)
                if k == 4:
                    full(1)
                if k == 5:
                    split_lo(1, 0, 1)
            v.wait_ge(w_lo_ok, KT)
            v.memset(raw[0][:, :, 0:HALO], 0.0).then_inc(halo_ok, 1)

            def convolve(b, i, par, g):
                v.wait_ge(evac, 4 + G * b + g + 1)
                if g == 0:
                    v.wait_ge(halo_ok, b + 1)
                    v.wait_ge(stored[par], 16 * (i + 1))
                out = act[par][:, g, :]
                done = TAPS * (G * b + g)
                v.tensor_scalar(out, raw[par][:, g, 0:N], taps[:, 0, g:g + 1], None, ALU.mult).then_inc(conv, 1)
                for j in range(1, TAPS):
                    v.wait_ge(conv, done + j)
                    v.scalar_tensor_tensor(out, raw[par][:, g, j:j + N], taps[:, j, g:g + 1], out,
                                           ALU.mult, ALU.add).then_inc(conv, 1)

            def decays(b, gates, n):
                at = V_AB * b
                v.wait_ge(ab_ok, b + 1)
                v.tensor_scalar(xa[:, :], psAB[0:2 * HA, 0:N], dt_b[:, :], None, ALU.add).then_inc(ab_v, 1)
                v.wait_ge(ab_v, at + 1)
                v.tensor_scalar(nx[:, :], xa[:, :], -1.0, None, ALU.mult).then_inc(ab_v, 1)
                v.wait_ge(ab_v, at + 2)
                v.tensor_tensor(na[:, :], xa[:, :], nx[:, :], ALU.min).then_inc(ab_v, 1)
                v.wait_ge(ab_s, S_AB * b + 1)
                v.tensor_scalar(w[:, :], u[:, :], 1.0, None, ALU.add).then_inc(ab_v, 1)
                v.wait_ge(ab_v, at + 4)
                v.scalar_tensor_tensor(c[:, :], w[:, :], -1.0, u[:, :], ALU.add, ALU.subtract).then_inc(ab_v, 1)
                v.wait_ge(ab_v, at + 5)
                v.wait_ge(ab_s, S_AB * b + 3)
                v.tensor_tensor(sp_[:, :], ln_w[:, :], c[:, :], ALU.subtract).then_inc(ab_v, 1)
                v.wait_ge(ab_v, at + 6)
                v.scalar_tensor_tensor(rx[:, :], xa[:, :], 0.0, sp_[:, :], ALU.max, ALU.add).then_inc(ab_v, 1)
                v.wait_ge(ab_v, at + 7)
                v.tensor_scalar(g_[:, :], rx[:, :], rate[:, :], -1.0, ALU.mult, ALU.mult).then_inc(ab_v, 1)
                v.wait_ge(ab_v, at + 8)
                v.wait_ge(ab_stored, 32 * (b + 1))
                v.tensor_tensor_scan(gc[:, :], gates[:, :], g_[:, :], 0.0, ALU.mult, ALU.add).then_inc(ab_v, 1)
                v.tensor_scalar(bden[:, :], en[:, :], 1.0, None, ALU.add).then_inc(ab_v, 1)
                v.wait_ge(ab_v, at + 10)
                v.reciprocal(beta[:, :], bden[:, :]).then_inc(ab_v, 1)

            v.wait_ge(rated, 1)
            with v.Fori(0, BLOCKS // 2) as i:
                for par in range(2):
                    b = 2 * i + par
                    for g in range(G):
                        convolve(b, i, par, g)
                        if g == 3:
                            full(2 * b + 2)
                        if g == 4:
                            split_lo(2 * b + 2, 1 - par, 0)
                        if g == 8:
                            full(2 * b + 3)
                        if g == 9:
                            split_lo(2 * b + 3, 1 - par, 1)
                    decays(b, gate, N)
            decays(BLOCKS, gate_s, P)


def project_b(nc, d, s):
    D, KT = s.D, s.D // P
    TILES = s.SEQ // P
    W = s.HB * s.DB
    SEG = 5
    ZA, Q, K, V, ZB = range(SEG)
    FIRST = s.QKV + 2 * s.HA
    H, DB = s.HB, s.DB
    with ExitStack() as stack:
        ph = Phase(nc, stack)
        w_hi = ph.sb("b_w_hi", [P, KT, SEG * W], F32R)
        w_lo = ph.sb("b_w_lo", [P, KT, SEG * W], F32R)
        x_raw = [ph.sb(f"b_x{i}", [P, D]) for i in range(2)]
        squares = ph.sb("b_squares", [P, D], mybir.dt.bfloat16)
        x_full = ph.sb("b_x_full", [P, KT, P])
        xT_hi = [ph.sb(f"b_xT_hi{i}", [P, KT, P], F32R) for i in range(2)]
        xT_lo = [ph.sb(f"b_xT_lo{i}", [P, KT, P], F32R) for i in range(2)]
        rows = ph.sb("b_rows", [P, SEG, W])
        HALF = SEG * W // 2
        spare = ph.sb("b_spare", [P, HALF])
        head_sq = [spare[:, i * W:(i + 1) * W] for i in range(2)]
        head_ms = [ph.sb(f"b_head_ms{i}", [P, H]) for i in range(2)]
        head_var = [ph.sb(f"b_head_var{i}", [P, H]) for i in range(2)]
        head_rstd = [ph.sb(f"b_head_rstd{i}", [P, H]) for i in range(2)]
        norm_g = ph.sb("b_norm_g", [P, 2, DB])
        lnT = ph.sb("b_lnT", [P, KT])
        ident = ph.sb("b_ident", [P, P])
        ssq = ph.sb("b_ssq", [P, 2])
        var = ph.sb("b_var", [P, 2])
        rstd = ph.sb("b_rstd", [P, 2])
        neg_half = ph.sb("b_neg_half", [P, H])

        psT = ph.ps("b_psT", [P, KT * P])
        psP = [ph.ps(f"b_psP{i}", [P, W]) for i in range(SEG)]

        consts = ph.sem("b_consts")
        filled = ph.sem("b_filled")
        w_in = [ph.sem(f"b_w_in{k}") for k in range(2 * KT)]
        w_hi_ok = ph.sem("b_w_hi_ok")
        w_lo_ok = ph.sem("b_w_lo_ok")
        x_in = [ph.sem(f"b_x_in{i}") for i in range(2)]
        ssq_ok = ph.sem("b_ssq_ok")
        var_ok = ph.sem("b_var_ok")
        rstd_ok = ph.sem("b_rstd_ok")
        scaled = ph.sem("b_scaled")
        xT_ps = ph.sem("b_xT_ps")
        full_ok = ph.sem("b_full_ok")
        hi_ok = ph.sem("b_hi_ok")
        lo_ok = ph.sem("b_lo_ok")
        prod = ph.sem("b_prod")
        read = [ph.sem(f"b_read{i}") for i in range(SEG)]
        sq_ok = ph.sem("b_sq_ok")
        ms_ok = ph.sem("b_ms_ok")
        head_var_ok = ph.sem("b_head_var_ok")
        head_rstd_ok = ph.sem("b_head_rstd_ok")
        gained = ph.sem("b_gained")
        stored = ph.sem("b_stored")

        flat = rows[:, :, :].rearrange("p s n -> p (s n)")
        stages = [flat[:, 0:HALF], flat[:, HALF:], spare[:, :]]
        parts_hi, parts_lo = ([w[:, k, h * HALF:(h + 1) * HALF] for k in range(KT) for h in range(2)] for w in (w_hi, w_lo))
        block = stack.enter_context(nc.Block())

        @block.sync
        def _(sp):
            with nc.allow_non_contiguous_dma(reason="small per-channel constants, once"):
                sp.dma_start(lnT[:, :], d.ln_g.rearrange("(k p) -> p k", p=P)).then_inc(consts, 16)
            for n, g in enumerate((d.q_g, d.k_g)):
                sp.dma_start(norm_g[:, n, :], g.partition_broadcast(P)).then_inc(consts, 16)
            for a in range(2):
                sp.dma_start(x_raw[a][:, :], d.x_p[a * P:(a + 1) * P, :]).then_inc(x_in[a], 16)
            for k in range(2 * KT):
                at = FIRST + k % 2 * HALF
                load_weight(sp, k, stages, d.w_in[k // 2 * P:(k // 2 + 1) * P, at:at + HALF], w_in, w_lo_ok)
            sp.wait_ge(xT_ps, 1)
            sp.dma_start(x_raw[0][:, :], d.x_p[2 * P:3 * P, :]).then_inc(x_in[0], 16)

            def tile_io(t, par, src):
                if src is not None:
                    sp.wait_ge(xT_ps, t + 2)
                    sp.dma_start(x_raw[1 - par][:, :], src).then_inc(x_in[1 - par], 16)
                waits_apart(sp, (consts, 16), [(read[seg], t + 2) for seg in (ZA, V, ZB)])
                sp.wait_ge(gained, 2 * (t + 1))
                sp.dma_start(d.rows_b[bass.ds(t * P, P), :], flat).then_inc(stored, 16)

            with sp.Fori(0, TILES // 2 - 2) as i:
                for par in range(2):
                    t = 2 * i + par
                    tile_io(t, par, d.x_p[bass.ds((t + 3) * P, P), :])
            tile_io(TILES - 4, 0, d.x_p[(TILES - 1) * P:TILES * P, :])
            tile_io(TILES - 3, 1, d.x_s)
            tile_io(TILES - 2, 0, None)
            tile_io(TILES - 1, 1, None)
            tile_io(TILES, 0, None)
            sp.wait_ge(stored, 16 * (TILES + 2))

        @block.gpsimd
        def _(pool):
            identity(pool, ident, filled)
            pool.memset(neg_half[:, :], -0.5).then_inc(filled, 1)
            pool.wait_ge(filled, 3)

            def norm(t, a):
                waits_apart(pool, (filled, 3), [(ssq_ok, t + 1)])
                pool.tensor_scalar(var[:, a:a + 1], ssq[:, a:a + 1], 1.0 / D, EPS, ALU.mult, ALU.add).then_inc(var_ok, 1)
                pool.wait_ge(var_ok, t + 1)
                pool.tensor_tensor(rstd[:, a:a + 1], var[:, a:a + 1], neg_half[:, 0:1], ALU.pow).then_inc(rstd_ok, 1)

            def head_norms(t):
                for n in range(2):
                    waits_apart(pool, (filled, 3), [(ms_ok, 2 * t + n + 1)])
                    pool.tensor_scalar(head_var[n][:, :], head_ms[n][:, :], 1.0 / DB, EPS, ALU.mult, ALU.add)\
                        .then_inc(head_var_ok, 1)
                    pool.wait_ge(head_var_ok, 2 * t + n + 1)
                    pool.tensor_tensor(head_rstd[n][:, :], head_var[n][:, :], neg_half[:, :], ALU.pow)\
                        .then_inc(head_rstd_ok, 1)

            norm(0, 0)
            with pool.Fori(0, TILES // 2) as i:
                for par in range(2):
                    t = 2 * i + par
                    norm(t + 1, 1 - par)
                    head_norms(t)
            head_norms(TILES)

        @block.scalar
        def _(e):
            def square(t, n, a, first=False):
                e.wait_ge(x_in[a], 16 * n)
                if not first:
                    e.wait_ge(ssq_ok, t)
                e.activation(squares[:, :], x_raw[a][:, :], ACT.Square, accum_out=ssq[:, a:a + 1]).then_inc(ssq_ok, 1)

            def scale(t, a):
                e.wait_ge(rstd_ok, t + 1)
                e.activation(x_raw[a][:, :], x_raw[a][:, :], ACT.Copy, scale=rstd[:, a:a + 1]).then_inc(scaled, 1)

            def split_hi(t, par):
                e.wait_ge(full_ok, t + 1)
                e.activation(xT_hi[par][:, :, :], x_full[:, :, :], ACT.Copy).then_inc(hi_ok, 1)

            square(0, 1, 0, first=True)
            scale(0, 0)
            for k in range(KT):
                for n in (2 * k, 2 * k + 1):
                    weight_hi(e, n, stages, parts_hi, w_in, w_hi_ok)
                if k == 0:
                    split_hi(0, 0)

            def run_tile(t, i, par, tail=False):
                def take(seg, func):
                    e.wait_ge(prod, SEG * t + seg + 1)
                    e.activation(rows[:, seg, :], psP[seg][:, :], func).then_inc(read[seg], 1)

                if not tail:
                    square(t + 1, i + 1 + par, 1 - par)
                    scale(t + 1, 1 - par)
                e.wait_ge(stored, 16 * (t + 1))
                take(ZA, ACT.Silu)
                for n, seg in enumerate((Q, K)):
                    e.wait_ge(prod, SEG * t + seg + 1)
                    e.activation(head_sq[n], psP[seg][:, :], ACT.Square).then_inc(sq_ok, 1)
                if not tail:
                    split_hi(t + 1, 1 - par)
                take(V, ACT.Copy)
                take(ZB, ACT.Silu)

            with e.Fori(0, TILES // 2) as i:
                for par in range(2):
                    run_tile(2 * i + par, i, par)
            run_tile(TILES, TILES // 2, 0, tail=True)

        @block.tensor
        def _(pe):
            pe.wait_ge(filled, 2)

            def transposes(t, a, first=False):
                pe.wait_ge(scaled, t + 1)
                if not first:
                    pe.wait_ge(full_ok, t)
                for k in range(KT):
                    last = nc.tensor.transpose(psT[:, k * P:(k + 1) * P], x_raw[a][:, k * P:(k + 1) * P], ident[:, :])
                last.then_inc(xT_ps, 1)

            transposes(0, 0, first=True)
            pe.wait_ge(lo_ok, 1)
            for seg in range(SEG):
                pe.wait_ge(read[seg], 1)
            for k in range(KT):
                pe.wait_ge(w_lo_ok, 2 * k + 2)
                for seg in range(SEG):
                    cols = slice(seg * W, (seg + 1) * W)
                    last = matmul3(nc, psP[seg][:, :], xT_hi[0][:, k, :], xT_lo[0][:, k, :], w_hi[:, k, cols],
                                   w_lo[:, k, cols], k == 0, k == KT - 1)
                    if k == KT - 1:
                        last.then_inc(prod, 1)
                if k == 1:
                    transposes(1, 1)

            def run_tile(t, par, tail=False):
                pe.wait_ge(lo_ok, t + 1)
                for seg in range(SEG):
                    pe.wait_ge(read[seg], t + 1)
                    cols = slice(seg * W, (seg + 1) * W)
                    for k in range(KT):
                        last = matmul3(nc, psP[seg][:, :], xT_hi[par][:, k, :], xT_lo[par][:, k, :], w_hi[:, k, cols],
                                       w_lo[:, k, cols], k == 0, k == KT - 1)
                    last.then_inc(prod, 1)
                    if seg == 1 and not tail:
                        transposes(t + 1, 1 - par)

            run_tile(1, 1)
            with pe.Fori(0, TILES // 2 - 1) as i:
                for par in range(2):
                    run_tile(2 * i + (2 + par), par)
            run_tile(TILES, 0, tail=True)

        @block.vector
        def _(v):
            for seg in range(SEG):
                v.sem_inc(read[seg], 1)
            v.sem_inc(stored, 16)
            v.wait_ge(consts, 48)

            def full(t, first=False):
                v.wait_ge(xT_ps, t + 1)
                if not first:
                    v.wait_ge(lo_ok, t)
                v.tensor_tensor(x_full[:, :, :], psT[:, :].rearrange("p (k n) -> p k n", k=KT),
                                lnT[:, :].unsqueeze(2).to_broadcast([P, KT, P]), ALU.mult).then_inc(full_ok, 1)

            def split_lo(t, par):
                v.wait_ge(hi_ok, t + 1)
                v.tensor_tensor(xT_lo[par][:, :, :], x_full[:, :, :], xT_hi[par][:, :, :].bitcast(F32),
                                ALU.subtract).then_inc(lo_ok, 1)

            for k in range(KT):
                if k == 0:
                    full(0, first=True)
                for n in (2 * k, 2 * k + 1):
                    weight_lo(v, n, stages, parts_hi, parts_lo, w_hi_ok, w_lo_ok)
                if k == 0:
                    split_lo(0, 0)

            def run_tile(t, par, tail=False):
                def head_sums(n):
                    v.wait_ge(sq_ok, 2 * t + n + 1)
                    v.tensor_reduce(head_ms[n][:, :], head_sq[n].rearrange("p (h c) -> p h c", h=H), AX.X,
                                    ALU.add).then_inc(ms_ok, 1)

                def normalise(n, seg):
                    out = rows[:, seg, :].rearrange("p (h c) -> p h c", h=H)
                    v.wait_ge(head_rstd_ok, 2 * t + n + 1)
                    if n == 0:
                        v.wait_ge(stored, 16 * (t + 1))
                    v.tensor_tensor(out, psP[seg][:, :].rearrange("p (h c) -> p h c", h=H),
                                    head_rstd[n][:, :].unsqueeze(2).to_broadcast([P, H, DB]), ALU.mult)\
                        .then_inc(read[seg], 1)
                    v.wait_ge(read[seg], t + 2)
                    v.tensor_tensor(out, out, norm_g[:, n:n + 1, :].to_broadcast([P, H, DB]), ALU.mult)\
                        .then_inc(gained, 1)

                head_sums(0)
                if not tail:
                    full(t + 1)
                head_sums(1)
                normalise(0, Q)
                if not tail:
                    split_lo(t + 1, 1 - par)
                normalise(1, K)

            with v.Fori(0, TILES // 2) as i:
                for par in range(2):
                    run_tile(2 * i + par, par)
            run_tile(TILES, 0, tail=True)


def sample_conv(nc, d, s):
    G, TAPS, HALO = s.QKV // P, s.CONVW, s.CONVW - 1
    NS, TS = s.DECB, s.DECT
    R = NS * HALO
    BANK = 512
    with ExitStack() as stack:
        ph = Phase(nc, stack)
        xs = ph.sb("c_xs", [P, G, NS, HALO + TS])
        fresh = ph.sb("c_fresh", [P, G, P])
        last = ph.sb("c_last", [P, G, HALO])
        newest = ph.sb("c_newest", [P, G, R])
        acts = ph.sb("c_acts", [P, G, P])
        taps = ph.sb("c_taps", [P, TAPS, G])
        old_rows = ph.sb("c_old_rows", [R, s.QKV])
        out_s = ph.sb("c_out_s", [R, s.QKV])
        out_p = ph.sb("c_out_p", [HALO, s.QKV])
        ident = ph.sb("c_ident", [P, P])
        ps_old = ph.ps("c_ps_old", [P, G, R])
        ps_s = [ph.ps(f"c_ps_s{i}", [P, BANK]) for i in range(3)]
        ps_p = [ph.ps(f"c_ps_p{i}", [P, BANK]) for i in range(3)]
        loaded = ph.sem("c_loaded")
        filled = ph.sem("c_filled")
        old_T = ph.sem("c_old_T")
        placed = ph.sem("c_placed")
        conv = ph.sem("c_conv")
        silu = ph.sem("c_silu")
        rows_ps = ph.sem("c_rows_ps")
        rows_ok = ph.sem("c_rows_ok")
        stored = ph.sem("c_stored")
        block = stack.enter_context(nc.Block())

        @block.sync
        def _(sp):
            with nc.allow_non_contiguous_dma(reason="small per-channel constants, once"):
                for j in range(TAPS):
                    sp.dma_start(taps[:, j, :], d.conv_w[j, :].rearrange("(g p) -> p g", p=P)).then_inc(loaded, 16)
            sp.dma_start(old_rows[:, :], d.state_conv.rearrange("b t c -> (b t) c")).then_inc(loaded, 16)
            sp.dma_start(fresh[:, :, :], d.rawT_s.rearrange("(g p) t -> p g t", p=P)).then_inc(loaded, 16)
            sp.dma_start(last[:, :, :], d.lastT.rearrange("(g p) t -> p g t", p=P)).then_inc(loaded, 16)
            sp.wait_ge(silu, 1)
            sp.dma_start(d.qkvT[:, s.SEQ:s.SEQ + P].rearrange("(g p) t -> p g t", p=P), acts[:, :, :]).then_inc(stored, 16)
            sp.wait_ge(rows_ok, 6)
            sp.dma_start(d.conv_s, out_s[:, :]).then_inc(stored, 16)
            sp.dma_start(d.conv_p, out_p[:, :]).then_inc(stored, 16)
            sp.wait_ge(stored, 48)

        @block.gpsimd
        def _(pool):
            identity(pool, ident, filled)

        @block.tensor
        def _(pe):
            pe.wait_ge(filled, 2)
            pe.wait_ge(loaded, 16 * (TAPS + 3))
            for g in range(G):
                t = nc.tensor.transpose(ps_old[:, g, :], old_rows[:, g * P:(g + 1) * P], ident[0:R, 0:R])
            t.then_inc(old_T, 1)
            pe.wait_ge(placed, 3)
            for g in range(G):
                at = slice(g % 4 * P, (g % 4 + 1) * P)
                nc.tensor.transpose(ps_s[g // 4][0:R, at], newest[:, g, :], ident[:, :])
                t = nc.tensor.transpose(ps_p[g // 4][0:HALO, at], last[:, g, :], ident[:, :])
            t.then_inc(rows_ps, 1)

        @block.vector
        def _(v):
            v.wait_ge(loaded, 16 * (TAPS + 3))
            v.wait_ge(old_T, 1)
            for g in range(G):
                v.tensor_copy(xs[:, g, :, 0:HALO], ps_old[:, g, :].rearrange("p (b t) -> p b t", b=NS))
            v.tensor_copy(newest[:, :, :].rearrange("p g (b t) -> p (g b) t", b=NS),
                          fresh[:, :, :].rearrange("p g (b t) -> p (g b) t", b=NS)[:, :, TS - HALO:]).then_inc(placed, 1)
            v.drain().then_inc(placed, 1)
            for g in range(G):
                v.tensor_copy(xs[:, g, :, HALO:], fresh[:, g, :].rearrange("p (b t) -> p b t", b=NS))
            v.drain().then_inc(placed, 1)
            v.wait_ge(placed, 3)
            for j in range(TAPS):
                if j:
                    v.wait_ge(conv, G * j)
                for g in range(G):
                    out = acts[:, g, :].rearrange("p (b t) -> p b t", b=NS)
                    if j == 0:
                        v.tensor_scalar(out, xs[:, g, :, 0:TS], taps[:, 0, g:g + 1], None, ALU.mult).then_inc(conv, 1)
                    else:
                        v.scalar_tensor_tensor(out, xs[:, g, :, j:j + TS], taps[:, j, g:g + 1], out, ALU.mult,
                                               ALU.add).then_inc(conv, 1)

        @block.scalar
        def _(e):
            e.wait_ge(conv, G * TAPS)
            e.activation(acts[:, :, :], acts[:, :, :], ACT.Silu).then_inc(silu, 1)
            e.wait_ge(rows_ps, 1)
            for j in range(3):
                e.activation(out_s[:, j * BANK:(j + 1) * BANK], ps_s[j][0:R, :], ACT.Copy).then_inc(rows_ok, 1)
                e.activation(out_p[:, j * BANK:(j + 1) * BANK], ps_p[j][0:HALO, :], ACT.Copy).then_inc(rows_ok, 1)


M_NEG, M_NEG_S, M_EYE, M_BASE, M_LEVEL, M_OWN = 0, 1, 2, 3, 4, 10
LEVELS = (2, 4, 8, 16, 32, 64)
BIG = 1e30


class Tile:

    def __init__(self, t, b, n, m=3):
        self.t, self.b, self.n, self.m = t, b, n, m

    def plus(self, k):
        return Tile(self.t + k, (self.b + k) % self.m, self.n + (self.b + k) // self.m, self.m)

    def next(self):
        return self.plus(1)

    def prev(self):
        return self.plus(-1)

    def first(self):
        return isinstance(self.t, int) and self.t == 0


def delta_masks(stream):
    j, i = np.meshgrid(np.arange(P), np.arange(P), indexing="ij")

    def level(b):
        return ((i // (2 * b) == j // (2 * b)) & (i // b % 2 == 1) & (j // b % 2 == 0)).astype(np.float32)

    ok = j <= i
    tables = [np.where(ok, 0, -BIG), np.where(ok & (i // stream == j // stream), 0, -BIG), np.eye(P), -level(1)]
    tables += [level(b) for b in LEVELS]
    tables += [j // stream == i]
    return np.ascontiguousarray(np.stack(tables, 1).astype(np.float32))


def delta(nc, d, s):
    NT = s.SEQ // P
    H, C = s.HA, s.DV
    PAIRS, GH = H // 2, H // 2
    W = H * C
    NL = len(LEVELS)
    SETS = [("T", -1, 0), ("T", -1, 1)]
    for lv in range(NL):
        for kind in ("P", "XT") + (("T",) if lv < NL - 1 else ()):
            SETS += [(kind, lv, 0), (kind, lv, 1)]
    NSETS = len(SETS)
    assert NSETS % 4 == 0
    S_SETS = [x for x in SETS if x[0] != "XT"]
    V_SETS = [x for x in SETS if x[0] == "XT"]
    NS_, NV_ = len(S_SETS), len(V_SETS)

    with ExitStack() as stack:
        ph = Phase(nc, stack)

        def three(name, shape):
            return [ph.sb(f"d_{name}{i}", shape) for i in range(3)]

        masks = ph.sb("d_masks", [P, M_LEVEL + NL, P])
        ident = ph.sb("d_ident", [P, P])
        conv_T = three("conv_T", [P, 3 * PAIRS, P])
        gcB = three("gcB", [P, H, P])
        ab = three("ab", [2 * H, P])
        za = three("za", [P, W])
        gain = ph.sb("d_gain", [P, C])
        exponent = ph.sb("d_exponent", [P, 2 * H])
        sq = ph.sb("d_sq", [P, 2, W])
        ssq = ph.sb("d_ssq", [P, 2 * H])
        var = ph.sb("d_var", [P, 2 * H])
        rn = ph.sb("d_rn", [P, 2 * H])
        gb = three("gb", [P, 2 * H])
        eg = three("eg", [P, H])
        bg = three("bg", [P, H])
        td = ph.sb("d_td", [P, H])
        et = three("et", [P, H])
        gt = three("gt", [P, H])
        qn = ph.sb("d_qn", [P, W])
        kn = three("kn", [P, W])
        kb = ph.sb("d_kb", [P, W])
        vb = three("vb", [P, W])
        KT = three("KT", [P, PAIRS, P])
        QT = three("QT", [P, PAIRS, P])
        right = ph.sb("d_right", [P, PAIRS, 4, P])
        dd = ph.sb("d_dd", [P, H, P])
        DT = ph.sb("d_DT", [P, H, P])
        NQ = three("NQ", [P, PAIRS, 4, P])
        NB = ph.sb("d_NB", [P, NL, H, P])
        base = ph.sb("d_base", [P, H, P])
        TT = three("TT", [P, H, P])
        T = ph.sb("d_T", [P, H, P])
        P1 = ph.sb("d_P1", [P, H, P])
        S = three("S", [P, PAIRS, P])
        r1 = ph.sb("d_r1", [P, W])
        r = ph.sb("d_r", [P, W])
        vn = ph.sb("d_vn", [P, W])
        vg = ph.sb("d_vg", [P, W])
        sgt = ph.sb("d_sgt", [P, PAIRS, C])
        o = ph.sb("d_o", [P, W])
        osq = ph.sb("d_osq", [P, W])
        oss = ph.sb("d_oss", [P, H])
        ovar = ph.sb("d_ovar", [P, H])
        orn = ph.sb("d_orn", [P, H])
        out = three("out", [P, W])

        ps_l = [ph.ps(f"d_ps_l{i}", [P, 512]) for i in range(4)]
        ps_m = [ph.ps(f"d_ps_m{i}", [P, 512]) for i in range(4)]

        consts = ph.sem("d_consts")
        filled = ph.sem("d_filled")
        cleared = ph.sem("d_cleared")
        t_rows = ph.sem("d_t_rows")
        v_gb = ph.sem("d_v_gb")
        s_sq = ph.sem("d_s_sq")
        v_ssq = ph.sem("d_v_ssq")
        g_var = ph.sem("d_g_var")
        g_rn = ph.sem("d_g_rn")
        s_eg = ph.sem("d_s_eg")
        v_td = ph.sem("d_v_td")
        s_et = ph.sem("d_s_et")
        v_bg = ph.sem("d_v_bg")
        v_qn = ph.sem("d_v_qn")
        v_kn = ph.sem("d_v_kn")
        v_kb = ph.sem("d_v_kb")
        v_vb = ph.sem("d_v_vb")
        t_back = ph.sem("d_t_back")
        s_kt = ph.sem("d_s_kt")
        v_kbt = ph.sem("d_v_kbt")
        s_qt = ph.sem("d_s_qt")
        v_qt = ph.sem("d_v_qt")
        v_dd = ph.sem("d_v_dd")
        g_dm = ph.sem("d_g_dm")
        s_dt = ph.sem("d_s_dt")
        t_c = ph.sem("d_t_c")
        v_c = ph.sem("d_v_c")
        g_nb = ph.sem("d_g_nb")
        v_base = ph.sem("d_v_base")
        t_l = ph.sem("d_t_l")
        l_s = ph.sem("d_l_s")
        l_v = ph.sem("d_l_v")
        t_ks = ph.sem("d_t_ks")
        v_r1 = ph.sem("d_v_r1")
        v_r = ph.sem("d_v_r")
        t_v = ph.sem("d_t_v")
        s_vn = ph.sem("d_s_vn")
        v_vg = ph.sem("d_v_vg")
        t_ds = ph.sem("d_t_ds")
        v_sgt = ph.sem("d_v_sgt")
        v_state = ph.sem("d_v_state")
        t_qs = ph.sem("d_t_qs")
        v_oq = ph.sem("d_v_oq")
        t_o = ph.sem("d_t_o")
        v_o = ph.sem("d_v_o")
        s_osq = ph.sem("d_s_osq")
        v_oss = ph.sem("d_v_oss")
        g_ovar = ph.sem("d_g_ovar")
        g_orn = ph.sem("d_g_orn")
        v_on = ph.sem("d_v_on")
        g_zg = ph.sem("d_g_zg")
        v_out = ph.sem("d_v_out")
        state_out = ph.sem("d_state_out")
        c_in = [ph.sem(f"d_c_in{i}") for i in range(3)]
        z_in = [ph.sem(f"d_z_in{i}") for i in range(3)]
        stored = [ph.sem(f"d_stored{i}") for i in range(3)]

        def heads(x):
            return x.rearrange("p (h c) -> p h c", h=H)

        def per_row(x):
            return x.unsqueeze(2).to_broadcast([P, H, C])

        def pipeline(eng, iteration):
            iteration(Tile(0, 0, 0), True, False)
            assert (NT - 2) % 3 == 0
            with eng.Fori(0, (NT - 2) // 3) as i:
                for u in range(3):
                    iteration(Tile(3 * i + (1 + u), (1 + u) % 3, i + (1 + u) // 3), True, True)
            iteration(Tile(NT - 1, (NT - 1) % 3, (NT - 1) // 3), False, True)

        def masked(eng, a, out, m):
            return eng.tensor_tensor(out.rearrange("p (a e) n -> p a e n", e=2), NQ[a.b][:, :, 0:2, :],
                                     masks[:, m:m + 1, :].unsqueeze(1).to_broadcast([P, PAIRS, 2, P]), ALU.mult)

        LAST = Tile(NT - 1, (NT - 1) % 3, (NT - 1) // 3)
        block = stack.enter_context(nc.Block())

        @block.sync
        def _(sp):
            sp.dma_start(masks[:, :, :], d.masks[:, 0:M_LEVEL + NL, :]).then_inc(consts, 16)
            sp.dma_start(gain[:, :], d.gdn_g.partition_broadcast(P)).then_inc(consts, 16)

            def load(a, t):
                at = bass.ds(t * P, P)
                sp.dma_start(conv_T[a][:, :, :], d.qkvT[:, at].rearrange("(g p) t -> p g t", p=P)).then_inc(c_in[a], 16)
                sp.dma_start(gcB[a][:, :, :], d.gcT[:, at].partition_broadcast(P)).then_inc(c_in[a], 16)
                sp.dma_start(ab[a][0:H, :], d.gcT[:, at]).then_inc(c_in[a], 16)
                sp.dma_start(ab[a][H:2 * H, :], d.betaT[:, at]).then_inc(c_in[a], 16)

            load(0, 0)
            load(1, 1)

            def store(a):
                sp.wait_ge(v_out, a.t + 4)
                sp.dma_start(d.mixed[bass.ds(a.t * P, P), 0:W], out[a.b][:, :]).then_inc(stored[a.b], 16)

            def iteration(a, pre, chain):
                if pre:
                    if chain:
                        sp.wait_ge(t_rows, 4 * a.t)
                        sp.wait_ge(s_et, a.t)
                        sp.wait_ge(v_dd, a.t)
                    load((a.b + 2) % 3, a.t + 2)
                sp.wait_ge(v_out, a.t + 1)
                sp.dma_start(za[a.b][:, :], d.rows_b[bass.ds(a.t * P, P), 0:W]).then_inc(z_in[a.b], 16)
                if chain:
                    store(a.prev())

            pipeline(sp, iteration)
            sp.wait_ge(v_state, 2 * NT + 2)
            for e in range(2):
                half = slice(e * C, (e + 1) * C)
                sp.dma_start(d.gdn_p.rearrange("(p e) k v -> e k p v", e=2)[e], S[LAST.b][half, :, half])\
                    .then_inc(state_out, 16)
            store(LAST)
            sp.wait_ge(state_out, 32)
            for b in range(3):
                sp.wait_ge(stored[b], 16 * (1 + (NT - b + 2) // 3))
                sp.wait_ge(c_in[b], 64 * ((NT + 1 - b + 2) // 3))

        @block.gpsimd
        def _(g):
            identity(g, ident, filled)
            g.memset(exponent[:, :], -0.5).then_inc(filled, 1)
            g.wait_ge(filled, 3)
            g.wait_ge(consts, 32)

            def norms(a):
                waits_apart(g, (filled, 3), [(v_ssq, 2 * (a.t + 1))])
                g.tensor_scalar(var[:, 0:H], ssq[:, 0:H], float(C), float(C) * EPS, ALU.mult, ALU.add).then_inc(g_var, 1)
                g.tensor_scalar(var[:, H:], ssq[:, H:], 1.0, EPS, ALU.mult, ALU.add).then_inc(g_var, 1)
                g.wait_ge(g_var, 2 * (a.t + 1))
                g.tensor_tensor(rn[:, :], var[:, :], exponent[:, :], ALU.pow).then_inc(g_rn, 1)

            def mask_decay(a):
                g.wait_ge(v_dd, a.t + 1)
                g.tensor_tensor(dd[:, :, :], dd[:, :, :], masks[:, M_NEG:M_NEG + 1, :].to_broadcast([P, H, P]), ALU.add)\
                    .then_inc(g_dm, 1)

            def level(a, lv):
                if not a.first():
                    g.wait_ge(t_l, NSETS * (a.t - 1) + SETS.index(("P", lv, 1)) + 1)
                elif lv == 0:
                    g.wait_ge(v_c, 4)
                masked(g, a, NB[:, lv, :, :], M_LEVEL + lv).then_inc(g_nb, 1)

            def gate(a):
                g.wait_ge(z_in[a.b], 16 * (a.n + 1))
                z = heads(za[a.b][:, :])
                g.tensor_tensor(z, z, gain[:, :].unsqueeze(1).to_broadcast([P, H, C]), ALU.mult).then_inc(g_zg, 1)

            def out_norm(a):
                waits_apart(g, (filled, 3), [(v_oss, a.t + 1)])
                g.tensor_scalar(ovar[:, :], oss[:, :], 1.0 / C, EPS, ALU.mult, ALU.add).then_inc(g_ovar, 1)
                g.wait_ge(g_ovar, a.t + 1)
                g.tensor_tensor(orn[:, :], ovar[:, :], exponent[:, 0:H], ALU.pow).then_inc(g_orn, 1)

            def iteration(a, pre, chain):
                if pre:
                    norms(a.next())
                level(a, 2)
                level(a, 3)
                if pre:
                    mask_decay(a.next())
                level(a, 4)
                if chain:
                    gate(a.prev())
                level(a, 5)
                if chain:
                    out_norm(a.prev())
                if pre:
                    g.wait_ge(v_c, 4 * (a.t + 2))
                    level(a.next(), 0)
                    level(a.next(), 1)

            first = Tile(0, 0, 0)
            norms(first)
            mask_decay(first)
            level(first, 0)
            level(first, 1)
            pipeline(g, iteration)
            gate(LAST)
            out_norm(LAST)

        @block.scalar
        def _(e):
            e.wait_ge(cleared, 4)

            def squares(a):
                for n in range(2):
                    e.wait_ge(t_rows, 4 * a.t + n + 1)
                    e.activation(sq[:, n, :], ps_m[n][:, :], ACT.Square).then_inc(s_sq, 1)

            def exps(a):
                e.wait_ge(v_gb, a.t + 1)
                e.activation(eg[a.b][:, :], gb[a.b][:, 0:H], ACT.Exp).then_inc(s_eg, 1)
                e.wait_ge(c_in[a.b], 64 * (a.n + 1))
                e.activation(gt[a.b][:, :], gcB[a.b][:, :, P - 1], ACT.Exp).then_inc(s_eg, 1)
                e.wait_ge(v_td, a.t + 1)
                e.activation(et[a.b][:, :], td[:, :], ACT.Exp).then_inc(s_et, 1)

            def take_keys(a):
                e.wait_ge(t_back, 3 * a.t + 1)
                e.activation(KT[a.b][:, :, :], ps_m[2][:, :].rearrange("p (a n) -> p a n", a=PAIRS), ACT.Copy).then_inc(s_kt, 1)

            def take_queries(a):
                e.wait_ge(t_back, 3 * a.t + 3)
                x = ps_m[0][:, :].rearrange("p (a n) -> p a n", a=PAIRS)
                e.activation(QT[a.b][:, :, :], x, ACT.Copy).then_inc(s_qt, 1)
                e.activation(right[0:C, :, 2, :], x[0:C], ACT.Copy).then_inc(s_qt, 1)

            def decay(a):
                e.wait_ge(g_dm, a.t + 1)
                e.activation(DT[:, :, :], dd[:, :, :], ACT.Exp).then_inc(s_dt, 1)

            def take(a, kind, lv, g):
                n = SETS.index((kind, lv, g))
                e.wait_ge(t_l, NSETS * a.t + n + 1)
                dst = T if kind == "T" else P1
                e.activation(dst[:, g * GH:(g + 1) * GH, :], ps_l[n % 4][:, :].rearrange("p (h n) -> p h n", h=GH),
                             ACT.Copy).then_inc(l_s, 1)

            def values(a):
                for n in range(2):
                    e.wait_ge(t_v, 2 * a.t + n + 1)
                    x = ps_m[n][:, :].rearrange("p (a m) -> p a m", a=2)
                    y = vn[:, n * W // 2:(n + 1) * W // 2].rearrange("p (a e c) -> p a e c", a=2, e=2)
                    for h in range(2):
                        e.activation(y[:, :, h, :], x[:, :, h * (P + C):h * (P + C) + C], ACT.Copy).then_inc(s_vn, 1)

            def out_square(a):
                e.wait_ge(v_o, 4 * a.t + 8)
                e.activation(osq[:, :], o[:, :], ACT.Square).then_inc(s_osq, 1)

            def iteration(a, pre, chain):
                take(a, "T", -1, 0)
                take(a, "T", -1, 1)
                if pre:
                    squares(a.next())
                for lv in range(NL):
                    if lv == 1 and pre:
                        exps(a.next())
                    if lv == 2 and chain:
                        values(a.prev())
                    if lv == 4 and pre:
                        take_keys(a.next())
                    take(a, "P", lv, 0)
                    take(a, "P", lv, 1)
                    if lv == 4 and pre:
                        take_queries(a.next())
                        decay(a.next())
                    if lv < NL - 1:
                        take(a, "T", lv, 0)
                        take(a, "T", lv, 1)
                    if lv == 3 and chain:
                        out_square(a.prev())

            first = Tile(0, 0, 0)
            squares(first)
            exps(first)
            take_keys(first)
            take_queries(first)
            decay(first)
            pipeline(e, iteration)
            values(LAST)
            out_square(LAST)

        @block.tensor
        def _(pe):
            pe.wait_ge(filled, 2)
            pe.wait_ge(cleared, 4)

            def rows(a, free):
                pe.wait_ge(c_in[a.b], 64 * (a.n + 1))
                for n in range(3):
                    if n == 2:
                        free(3)
                    free(n)
                    for p in range(PAIRS):
                        last = nc.tensor.transpose(ps_m[n][:, p * P:(p + 1) * P], conv_T[a.b][:, n * PAIRS + p, :], ident[:, :])
                    last.then_inc(t_rows, 1)
                nc.tensor.transpose(ps_m[3][:, 0:2 * H], ab[a.b][:, :], ident[0:2 * H, 0:2 * H]).then_inc(t_rows, 1)

            def back(a, chained):
                for n, src, there in ((2, kn[a.b], v_kn), (3, kb, v_kb), (0, qn, v_qn)):
                    pe.wait_ge(there, a.t + 1)
                    if n == 2:
                        pe.wait_ge(v_vb, a.t + 1)
                        if chained:
                            pe.wait_ge(v_o, 4 * a.t)
                    for p in range(PAIRS):
                        last = nc.tensor.transpose(ps_m[n][:, p * P:(p + 1) * P], src[:, p * P:(p + 1) * P], ident[:, :])
                    last.then_inc(t_back, 1)

            def products(a, chained):
                pe.wait_ge(s_kt, a.t + 1)
                pe.wait_ge(v_kbt, 2 * (a.t + 1))
                pe.wait_ge(s_qt, 2 * (a.t + 1))
                pe.wait_ge(v_qt, a.t + 1)
                if chained:
                    pe.wait_ge(v_state, 2 * (a.t - 1) + 2)
                for p, bank in enumerate((2, 3, 0, 1)):
                    nc.tensor.matmul(ps_m[bank][:, :], KT[a.b][:, p, :], right[:, p, :, :], start=True, stop=True)\
                        .then_inc(t_c, 1)

            def step(a, kind, lv, g):
                n = SETS.index((kind, lv, g))
                if kind == "P" and lv == 0 and not a.first():
                    pe.wait_ge(l_v, NV_ * (a.t - 1) + V_SETS.index(("XT", NL - 1, g)) + 1)
                if kind == "T" and lv < 0:
                    pe.wait_ge(v_base, 2 * (a.t + 1))
                elif kind == "T":
                    pe.wait_ge(l_v, NV_ * a.t + V_SETS.index(("XT", lv, g)) + 1)
                elif kind == "P":
                    if g == 0:
                        pe.wait_ge(g_nb, NL * a.t + lv + 1)
                    pe.wait_ge(l_s, NS_ * a.t + S_SETS.index(("T", lv - 1, g)) + 1)
                else:
                    pe.wait_ge(l_s, NS_ * a.t + S_SETS.index(("P", lv, g)) + 1)
                for j in range(GH):
                    h = g * GH + j
                    dst = ps_l[n % 4][:, j * P:(j + 1) * P]
                    if kind == "T":
                        last = nc.tensor.transpose(dst, TT[a.b][:, h, :], ident[:, :])
                    elif kind == "P":
                        last = nc.tensor.matmul(dst, NB[:, lv, h, :], T[:, h, :], start=True, stop=True)
                    else:
                        last = nc.tensor.matmul(dst, P1[:, h, :], TT[a.b][:, h, :], start=True, stop=True)
                last.then_inc(t_l, 1)

            def through_state(a, bank, left, done):
                for p in range(PAIRS):
                    last = nc.tensor.matmul(ps_m[bank][:, p * P:(p + 1) * P], left[a.b][:, p, :], S[(a.b + 2) % 3][:, p, :],
                                            start=True, stop=True)
                last.then_inc(done, 1)

            def per_head(left, rhs, banks, done):
                for n in range(2):
                    for j in range(GH):
                        h = n * GH + j
                        last = nc.tensor.matmul(ps_m[banks[n]][:, j * P:(j + 1) * P], left(h),
                                                rhs[:, h // 2 * P:(h // 2 + 1) * P], start=True, stop=True)
                    last.then_inc(done, 1)

            def keys_state(a, pre):
                if pre:
                    pe.wait_ge(v_gb, a.t + 3)
                else:
                    pe.wait_ge(v_c, 4 * NT)
                    pe.wait_ge(v_o, 4 * a.t + 4)
                pe.wait_ge(v_state, 2 * a.t + 2)
                through_state(a, 3, KT, t_ks)

            def new_values(a, pre):
                pe.wait_ge(v_r, a.t + 1)
                pe.wait_ge(l_v, NV_ * (a.t + 1))
                if pre:
                    pe.wait_ge(v_qn, a.t + 3)
                per_head(lambda h: TT[a.b][:, h, :], r, (0, 1), t_v)

            def new_state(a):
                pe.wait_ge(v_vg, a.t + 1)
                for p in range(PAIRS):
                    at = slice(p * P, (p + 1) * P)
                    last = nc.tensor.matmul(ps_m[1][:, at], kn[a.b][:, at], vg[:, at], start=True, stop=True)
                last.then_inc(t_ds, 1)

            def outputs(a, pre):
                if pre:
                    pe.wait_ge(v_vb, a.t + 3)
                through_state(a, 2, QT, t_qs)
                pe.wait_ge(s_vn, 4 * (a.t + 1))
                per_head(lambda h: NQ[a.b][:, h // 2, 2 + h % 2, :], vn, (3, 0), t_o)

            def iteration(a, pre, chain):
                step(a, "T", -1, 0)
                step(a, "T", -1, 1)
                if pre:
                    rows(a.next(), lambda n: pe.wait_ge(v_c, 4 * (a.t + 1)))
                for lv in range(NL):
                    if lv == 1 and chain:
                        keys_state(a.prev(), pre)
                    if lv == 2 and chain:
                        new_values(a.prev(), pre)
                    if lv == 3 and chain:
                        outputs(a.prev(), pre)
                        new_state(a.prev())
                    if lv == 4 and pre:
                        back(a.next(), chain)
                    step(a, "P", lv, 0)
                    step(a, "P", lv, 1)
                    step(a, "XT", lv, 0)
                    step(a, "XT", lv, 1)
                    if lv == 4 and pre:
                        products(a.next(), chain)
                    if lv < NL - 1:
                        step(a, "T", lv, 0)
                        step(a, "T", lv, 1)

            first = Tile(0, 0, 0)
            rows(first, lambda n: None)
            back(first, False)
            products(first, False)
            pipeline(pe, iteration)
            keys_state(LAST, False)
            new_values(LAST, False)
            new_state(LAST)
            outputs(LAST, False)

        @block.vector
        def _(v):
            v.memset(right[:, :, :, :], 0.0).then_inc(cleared, 1)
            for b in range(3):
                v.memset(S[b][:, :, :], 0.0).then_inc(cleared, 1)
                v.sem_inc(stored[b], 16)
            v.wait_ge(cleared, 4)
            for x, n in ((v_state, 2), (v_oq, 1), (v_o, 4), (v_out, 3)):
                v.sem_inc(x, n)

            def sums(a):
                v.wait_ge(t_rows, 4 * a.t + 4)
                v.tensor_copy(gb[a.b][:, :], ps_m[3][:, 0:2 * H]).then_inc(v_gb, 1)
                v.wait_ge(v_gb, a.t + 1)
                v.wait_ge(c_in[a.b], 64 * (a.n + 1))
                v.tensor_tensor(td[:, :], gcB[a.b][:, :, P - 1], gb[a.b][:, 0:H], ALU.subtract).then_inc(v_td, 1)
                for n in range(2):
                    v.wait_ge(s_sq, 2 * a.t + n + 1)
                    v.tensor_reduce(ssq[:, n * H:(n + 1) * H], heads(sq[:, n, :]), AX.X, ALU.add).then_inc(v_ssq, 1)

            def norms(a):
                v.wait_ge(g_rn, a.t + 1)
                v.tensor_tensor(heads(kn[a.b][:, :]), heads(ps_m[1][:, :]), per_row(rn[:, H:]), ALU.mult).then_inc(v_kn, 1)
                v.tensor_tensor(heads(qn[:, :]), heads(ps_m[0][:, :]), per_row(rn[:, 0:H]), ALU.mult).then_inc(v_qn, 1)

            def beta_values(a):
                v.wait_ge(t_rows, 4 * a.t + 3)
                v.tensor_tensor(heads(vb[a.b][:, :]), heads(ps_m[2][:, :]), per_row(gb[a.b][:, H:]), ALU.mult).then_inc(v_vb, 1)

            def beta_keys(a):
                v.wait_ge(t_back, 3 * a.t + 2)
                x = ps_m[3][:, :].rearrange("p (a n) -> p a n", a=PAIRS)
                v.tensor_copy(right[0:C, :, 0, :], x[0:C]).then_inc(v_kbt, 1)
                v.tensor_copy(right[C:, :, 1, :], x[C:]).then_inc(v_kbt, 1)
                v.wait_ge(s_qt, 2 * a.t + 1)
                v.tensor_copy(right[C:, :, 3, :], QT[a.b][C:, :, :]).then_inc(v_qt, 1)

            def betas(a):
                v.wait_ge(v_kn, a.t + 1)
                v.tensor_tensor(heads(kb[:, :]), heads(kn[a.b][:, :]), per_row(gb[a.b][:, H:]), ALU.mult).then_inc(v_kb, 1)
                v.tensor_tensor(dd[:, :, :], gcB[a.b][:, :, :], gb[a.b][:, 0:H].unsqueeze(2).to_broadcast([P, H, P]),
                                ALU.subtract).then_inc(v_dd, 1)
                v.wait_ge(s_eg, 2 * a.t + 1)
                v.tensor_tensor(bg[a.b][:, :], eg[a.b][:, :], gb[a.b][:, H:], ALU.mult).then_inc(v_bg, 1)

            def decayed(a):
                v.wait_ge(s_dt, a.t + 1)
                for p, bank in enumerate((2, 3, 0, 1)):
                    v.wait_ge(t_c, 4 * a.t + p + 1)
                    v.tensor_tensor(NQ[a.b][:, p, :, :].rearrange("p (x e) n -> p x e n", x=2),
                                    ps_m[bank][:, :].rearrange("p (x e n) -> p x e n", x=2, e=2),
                                    DT[:, 2 * p:2 * p + 2, :].unsqueeze(1).to_broadcast([P, 2, 2, P]), ALU.mult)\
                        .then_inc(v_c, 1)

            def start(a):
                v.wait_ge(v_c, 4 * (a.t + 1))
                masked(v, a, base[:, :, :], M_BASE).then_inc(v_base, 1)
                v.wait_ge(v_base, 2 * a.t + 1)
                v.tensor_tensor(TT[a.b][:, :, :], base[:, :, :], masks[:, M_EYE:M_EYE + 1, :].to_broadcast([P, H, P]),
                                ALU.add).then_inc(v_base, 1)

            def take(a, kind, lv, g):
                n = SETS.index((kind, lv, g))
                x = TT[a.b][:, g * GH:(g + 1) * GH, :]
                v.wait_ge(t_l, NSETS * a.t + n + 1)
                v.tensor_tensor(x, x, ps_l[n % 4][:, :].rearrange("p (h n) -> p h n", h=GH), ALU.subtract).then_inc(l_v, 1)

            def residual(a):
                v.wait_ge(t_ks, a.t + 1)
                v.wait_ge(v_bg, a.t + 1)
                v.tensor_tensor(heads(r1[:, :]), heads(ps_m[3][:, :]), per_row(bg[a.b][:, :]), ALU.mult).then_inc(v_r1, 1)
                v.wait_ge(v_r1, a.t + 1)
                v.tensor_tensor(r[:, :], vb[a.b][:, :], r1[:, :], ALU.subtract).then_inc(v_r, 1)

            def tail_values(a):
                v.wait_ge(s_vn, 4 * (a.t + 1))
                v.wait_ge(s_et, a.t + 1)
                v.tensor_tensor(heads(vg[:, :]), heads(vn[:, :]), per_row(et[a.b][:, :]), ALU.mult).then_inc(v_vg, 1)

            def state(a):
                old, new = S[(a.b + 2) % 3], S[a.b]
                v.wait_ge(v_state, 2 * a.t + 2)
                for e in range(2):
                    half = slice(e * C, (e + 1) * C)
                    v.tensor_tensor(sgt[half, :, :], old[half, :, half],
                                    gt[a.b][half, e::2].unsqueeze(2).to_broadcast([C, PAIRS, C]), ALU.mult).then_inc(v_sgt, 1)
                v.wait_ge(v_sgt, 2 * (a.t + 1))
                v.wait_ge(t_ds, a.t + 1)
                for e in range(2):
                    half = slice(e * C, (e + 1) * C)
                    x = ps_m[1][:, :].rearrange("p (a n) -> p a n", a=PAIRS)
                    v.tensor_tensor(new[half, :, half], sgt[half, :, :], x[half, :, half], ALU.add).then_inc(v_state, 1)

            def outputs(a):
                v.wait_ge(t_qs, a.t + 1)
                v.tensor_tensor(heads(o[:, :]), heads(ps_m[2][:, :]), per_row(eg[a.b][:, :]), ALU.mult).then_inc(v_oq, 1)
                v.wait_ge(v_oq, a.t + 2)
                for n, bank in enumerate((3, 0)):
                    v.wait_ge(t_o, 2 * a.t + n + 1)
                    x = ps_m[bank][:, :].rearrange("p (a m) -> p a m", a=2)
                    y = o[:, n * W // 2:(n + 1) * W // 2].rearrange("p (a e c) -> p a e c", a=2, e=2)
                    for h in range(2):
                        z = y[:, :, h, :]
                        v.tensor_tensor(z, z, x[:, :, h * (P + C):h * (P + C) + C], ALU.add).then_inc(v_o, 1)

            def out_sums(a):
                v.wait_ge(s_osq, a.t + 1)
                v.tensor_reduce(oss[:, :], heads(osq[:, :]), AX.X, ALU.add).then_inc(v_oss, 1)

            def finish(a):
                v.wait_ge(g_orn, a.t + 1)
                v.tensor_tensor(heads(o[:, :]), heads(o[:, :]), per_row(orn[:, :]), ALU.mult).then_inc(v_on, 1)
                v.wait_ge(v_on, a.t + 1)
                v.wait_ge(g_zg, a.t + 1)
                v.wait_ge(stored[a.b], 16 * (a.n + 1))
                v.tensor_tensor(out[a.b][:, :], o[:, :], za[a.b][:, :], ALU.mult).then_inc(v_out, 1)

            def iteration(a, pre, chain):
                before = ((), (residual,), (tail_values,), (outputs,), (out_sums,), ())
                ahead = ((sums,), (norms,), (beta_values,), (), (beta_keys,), (start,))
                behind = ((), (), (betas,), (), (decayed,), ())
                for lv in range(NL):
                    if chain:
                        for stage in before[lv]:
                            stage(a.prev())
                    if pre:
                        for stage in ahead[lv]:
                            stage(a.next())
                    take(a, "XT", lv, 0)
                    take(a, "XT", lv, 1)
                    if pre:
                        for stage in behind[lv]:
                            stage(a.next())
                    if lv == 3 and chain:
                        state(a.prev())
                if chain:
                    finish(a.prev())

            first = Tile(0, 0, 0)
            sums(first)
            norms(first)
            beta_values(first)
            betas(first)
            beta_keys(first)
            decayed(first)
            start(first)
            pipeline(v, iteration)
            residual(LAST)
            tail_values(LAST)
            state(LAST)
            outputs(LAST)
            out_sums(LAST)
            finish(LAST)


def after(steps, name):
    return steps.index(name) + 1


def delta_sample(nc, d, s):
    H, C = s.HA, s.DV
    PAIRS, GH = H // 2, H // 2
    W = H * C
    NS, TS = s.DECB, s.DECT
    NL = LEVELS.index(TS)
    HALVES = 2 * PAIRS
    HS = NS // 2

    T_STEPS = ["rows q", "rows k", "rows v", "K^T", "bK^T", "Q^T"] + [f"products {p}" for p in range(PAIRS)]
    T_STEPS += ["T 0", "T 1"] + [f"{k} {lv} {g}" for lv in range(NL) for k in ("P", "X", "XT") for g in range(2)]
    T_STEPS += ["KS^T", "QS^T", "KS", "QS", "V 0", "V 1", "O 0", "O 1"] + [f"dS {n}" for n in range(HALVES)]
    S_STEPS = ["squares q", "squares k", "eg", "gt", "et", "K^T", "bK^T 0", "bK^T 1", "Q^T", "Q^T 0", "Q^T 1", "D",
               "T 0", "T 1"] + [f"P {lv} {g}" for lv in range(NL) for g in range(2)]
    S_STEPS += ["KS^T", "QS^T"] + [f"V {n} {h}" for n in range(2) for h in range(2)] + ["squares o"]
    V_STEPS = ["ssq q", "ssq k", "kn", "qn", "kb", "vb", "dd", "td", "bg"] + [f"NQ {p}" for p in range(PAIRS)] + ["base", "TT"]
    V_STEPS += [f"{k} {lv} {g}" for lv in range(NL) for k in ("X", "XT") for g in range(2)]
    V_STEPS += ["bg KS", "r", "vg"] + [f"vg {b}" for b in range(NS)] + ["gt S 0", "gt S 1", "eg QS"]
    V_STEPS += [f"O {n} {h}" for n in range(2) for h in range(2)] + ["ssq o"]
    V_STEPS += [f"S {n} {e}" for n in range(HALVES) for e in range(2)] + ["on", "out"]
    G_STEPS = ["zeros", "ident", "exponent", "right 0", "state 0", "var q", "var k", "rn", "dd"]
    G_STEPS += [f"level {lv}" for lv in range(NL)] + ["gate", "var o", "rn o"]

    with ExitStack() as stack:
        ph = Phase(nc, stack)
        masks = ph.sb("e_masks", [P, M_OWN + 1, P])
        ident = ph.sb("e_ident", [P, P])
        conv_T = ph.sb("e_conv_T", [P, 3 * PAIRS, P])
        gcB = ph.sb("e_gcB", [P, H, P])
        gb = ph.sb("e_gb", [P, 2 * H])
        g_end = ph.sb("e_g_end", [P, H])
        za = ph.sb("e_za", [P, W])
        gain = ph.sb("e_gain", [P, C])
        exponent = ph.sb("e_exponent", [P, 2 * H])
        sq = ph.sb("e_sq", [P, 2, W])
        ssq, var, rn = (ph.sb(f"e_{k}", [P, 2 * H]) for k in ("ssq", "var", "rn"))
        eg, bg, td, et, oss, ovar, orn = (ph.sb(f"e_{k}", [P, H]) for k in ("eg", "bg", "td", "et", "oss", "ovar", "orn"))
        gt = ph.sb("e_gt", [P, H, NS])
        qn, kn, kb, vb, r1, r, vn, vg, o, osq, out = (ph.sb(f"e_{k}", [P, W]) for k in (
            "qn", "kn", "kb", "vb", "r1", "r", "vn", "vg", "o", "osq", "out"))
        KT, QT, KS, QS = (ph.sb(f"e_{k}", [P, PAIRS, P]) for k in ("KT", "QT", "KS", "QS"))
        right = ph.sb("e_right", [P, PAIRS, 4, P])
        dd, DT, base, TT, T, P1 = (ph.sb(f"e_{k}", [P, H, P]) for k in ("dd", "DT", "base", "TT", "T", "P1"))
        NQ = ph.sb("e_NQ", [P, PAIRS, 4, P])
        NB = ph.sb("e_NB", [P, NL, H, P])
        S = ph.sb("e_S", [P, PAIRS, NS, P])
        sgt = ph.sb("e_sgt", [P, PAIRS * NS, C])
        S_new = ph.sb("e_S_new", [P, PAIRS, NS, C])
        vgb = ph.sb("e_vgb", [P, NS, W])

        ps = [ph.ps(f"e_ps{i}", [P, 512]) for i in range(8)]
        conv_in = ph.sem("e_conv_in")
        loaded = ph.sem("e_loaded")
        states_in = ph.sem("e_states_in")
        t_ok = ph.sem("e_t_ok")
        s_ok = ph.sem("e_s_ok")
        v_ok = ph.sem("e_v_ok")
        g_ok = ph.sem("e_g_ok")
        stored = ph.sem("e_stored")
        LOADS = 6 + NS

        def for_t(eng, name):
            eng.wait_ge(t_ok, after(T_STEPS, name))

        def for_s(eng, name):
            eng.wait_ge(s_ok, after(S_STEPS, name))

        def for_v(eng, name):
            eng.wait_ge(v_ok, after(V_STEPS, name))

        def for_g(eng, name):
            eng.wait_ge(g_ok, after(G_STEPS, name))

        def heads(x):
            return x.rearrange("p (h c) -> p h c", h=H)

        def pairs(x):
            return x.rearrange("p (a n) -> p a n", a=PAIRS)

        def per_row(x):
            return x.unsqueeze(2).to_broadcast([P, H, C])

        def masked(eng, out, m):
            return eng.tensor_tensor(out.rearrange("p (a e) n -> p a e n", e=2), NQ[:, :, 0:2, :],
                                     masks[:, m:m + 1, :].unsqueeze(1).to_broadcast([P, PAIRS, 2, P]), ALU.mult)

        block = stack.enter_context(nc.Block())

        @block.sync
        def _(sp):
            at = slice(s.SEQ, s.SEQ + P)
            sp.dma_start(conv_T[:, :, :], d.qkvT[:, at].rearrange("(g p) t -> p g t", p=P)).then_inc(conv_in, 16)
            with nc.allow_non_contiguous_dma(reason="a row of decays and betas per token, once"):
                sp.dma_start(gb[:, 0:H], d.gcT[:, at].rearrange("h t -> t h")).then_inc(loaded, 16)
                sp.dma_start(gb[:, H:], d.betaT[:, at].rearrange("h t -> t h")).then_inc(loaded, 16)
                for b in range(NS):
                    end = s.SEQ + (b + 1) * TS - 1
                    sp.dma_start(g_end[b * TS:(b + 1) * TS, :], d.gcT[:, end].partition_broadcast(TS)).then_inc(loaded, 16)
            sp.dma_start(gcB[:, :, :], d.gcT[:, at].partition_broadcast(P)).then_inc(loaded, 16)
            sp.dma_start(masks[:, :, :], d.masks).then_inc(loaded, 16)
            sp.dma_start(gain[:, :], d.gdn_g.partition_broadcast(P)).then_inc(loaded, 16)
            sp.dma_start(za[:, :], d.rows_b[at, 0:W]).then_inc(loaded, 16)
            for_g(sp, "state 0")
            for p in range(PAIRS):
                for e in range(2):
                    sp.dma_start(S[e * C:(e + 1) * C, p, :, e * C:(e + 1) * C],
                                 d.state_gdn[:, 2 * p + e].rearrange("b k v -> k b v")).then_inc(states_in, 16)
            for_v(sp, f"S {HALVES - 1} 1")
            for p in range(PAIRS):
                sp.dma_start(d.gdn_s[:, 2 * p:2 * p + 2].rearrange("b e k v -> (e k) b v"), S_new[:, p, :, :])\
                    .then_inc(stored, 16)
            for_v(sp, "out")
            sp.dma_start(d.mixed[at, 0:W], out[:, :]).then_inc(stored, 16)
            sp.wait_ge(stored, 16 * (PAIRS + 1))

        @block.gpsimd
        def _(g):
            identity(g, ident, g_ok)
            g.memset(exponent[:, :], -0.5).then_inc(g_ok, 1)
            g.memset(right[:, :, :, :], 0.0).then_inc(g_ok, 1)
            g.memset(S[:, :, :, :], 0.0).then_inc(g_ok, 1)
            for_v(g, "ssq k")
            g.tensor_scalar(var[:, 0:H], ssq[:, 0:H], float(C), float(C) * EPS, ALU.mult, ALU.add).then_inc(g_ok, 1)
            g.tensor_scalar(var[:, H:], ssq[:, H:], 1.0, EPS, ALU.mult, ALU.add).then_inc(g_ok, 1)
            for_g(g, "var k")
            g.tensor_tensor(rn[:, :], var[:, :], exponent[:, :], ALU.pow).then_inc(g_ok, 1)
            for_v(g, "dd")
            g.tensor_tensor(dd[:, :, :], dd[:, :, :], masks[:, M_NEG_S:M_NEG_S + 1, :].to_broadcast([P, H, P]), ALU.add)\
                .then_inc(g_ok, 1)
            for_v(g, f"NQ {PAIRS - 1}")

            for lv in range(NL):
                masked(g, NB[:, lv, :, :], M_LEVEL + lv).then_inc(g_ok, 1)
            g.tensor_tensor(heads(za[:, :]), heads(za[:, :]), gain[:, :].unsqueeze(1).to_broadcast([P, H, C]), ALU.mult)\
                .then_inc(g_ok, 1)
            for_v(g, "ssq o")
            g.tensor_scalar(ovar[:, :], oss[:, :], 1.0 / C, EPS, ALU.mult, ALU.add).then_inc(g_ok, 1)
            for_g(g, "var o")
            g.tensor_tensor(orn[:, :], ovar[:, :], exponent[:, 0:H], ALU.pow).then_inc(g_ok, 1)

        @block.tensor
        def _(pe):
            pe.wait_ge(conv_in, 16)
            for_g(pe, "ident")

            def transposes(bank, src):
                for p in range(PAIRS):
                    last = nc.tensor.transpose(ps[bank][:, p * P:(p + 1) * P], src(p), ident[:, :])
                last.then_inc(t_ok, 1)

            def per_head(bank, g, left, rhs):
                for j in range(GH):
                    h = g * GH + j
                    last = nc.tensor.matmul(ps[bank][:, j * P:(j + 1) * P], left(h), rhs(h), start=True, stop=True)
                last.then_inc(t_ok, 1)

            for n in range(3):
                transposes(n, lambda p: conv_T[:, n * PAIRS + p, :])
            for bank, src, name in ((3, kn, "kn"), (4, kb, "kb"), (5, qn, "qn")):
                for_v(pe, name)
                transposes(bank, lambda p: src[:, p * P:(p + 1) * P])
            for_s(pe, "Q^T 1")
            for_v(pe, "vb")
            for p, bank in enumerate((0, 1, 2, 6)):
                nc.tensor.matmul(ps[bank][:, :], KT[:, p, :], right[:, p, :, :], start=True, stop=True).then_inc(t_ok, 1)
            for_v(pe, "TT")
            for g in range(2):
                per_head_T = [nc.tensor.transpose(ps[3 + g][:, j * P:(j + 1) * P], TT[:, g * GH + j, :], ident[:, :])
                              for j in range(GH)]
                per_head_T[-1].then_inc(t_ok, 1)
            for lv in range(NL):
                for_g(pe, f"level {lv}")
                for g in range(2):
                    if lv:
                        for_v(pe, f"X {lv - 1} {g}")
                    for_s(pe, f"T {g}")
                    per_head((5, 7)[g], g, lambda h: NB[:, lv, h, :], lambda h: T[:, h, :])
                for kind, banks in (("X", (0, 1)), ("XT", (2, 6))):
                    for g in range(2):
                        for_s(pe, f"P {lv} {g}")
                        if lv:
                            for_v(pe, f"XT {lv - 1} {g}")
                        if kind == "X":
                            per_head(banks[g], g, lambda h: TT[:, h, :], lambda h: P1[:, h, :])
                        else:
                            per_head(banks[g], g, lambda h: P1[:, h, :], lambda h: TT[:, h, :])
            pe.wait_ge(states_in, 16 * 2 * PAIRS)
            for bank, x in ((3, KT), (4, QT)):
                for p in range(PAIRS):
                    for b in range(NS):
                        at = slice(b * TS, (b + 1) * TS)
                        last = nc.tensor.matmul(ps[bank][:, p * P + b * TS:p * P + (b + 1) * TS], S[:, p, b, :], x[:, p, at],
                                                start=True, stop=True)
                last.then_inc(t_ok, 1)
            for bank, x, name in ((5, KS, "KS^T"), (7, QS, "QS^T")):
                for_s(pe, name)
                transposes(bank, lambda p: x[:, p, :])
            for_v(pe, "r")
            for_v(pe, f"XT {NL - 1} 1")
            for g in range(2):
                per_head(g, g, lambda h: TT[:, h, :], lambda h: r[:, h // 2 * P:(h // 2 + 1) * P])
            for_s(pe, "V 1 1")
            for g in range(2):
                per_head(g, g, lambda h: NQ[:, h // 2, 2 + h % 2, :], lambda h: vn[:, h // 2 * P:(h // 2 + 1) * P])
            for_v(pe, f"vg {NS - 1}")
            for n in range(HALVES):
                if n >= 4:
                    for_v(pe, f"S {n - 4} 1")
                p, b = n // 2, n % 2 * HS
                nc.tensor.matmul(ps[(2, 3, 4, 6)[n % 4]][:, :], kn[:, p * P:(p + 1) * P], vgb[:, b:b + HS, p * P:(p + 1) * P],
                                 start=True, stop=True).then_inc(t_ok, 1)

        @block.scalar
        def _(e):
            for n, name in enumerate("qk"):
                for_t(e, f"rows {name}")
                e.activation(sq[:, n, :], ps[n][:, :], ACT.Square).then_inc(s_ok, 1)
            e.wait_ge(loaded, 16 * LOADS)
            e.activation(eg[:, :], gb[:, 0:H], ACT.Exp).then_inc(s_ok, 1)
            e.activation(gt[:, :, :], gcB[:, :, TS - 1::TS], ACT.Exp).then_inc(s_ok, 1)
            for_v(e, "td")
            e.activation(et[:, :], td[:, :], ACT.Exp).then_inc(s_ok, 1)
            for_g(e, "right 0")
            for_t(e, "K^T")
            e.activation(KT[:, :, :], pairs(ps[3][:, :]), ACT.Copy).then_inc(s_ok, 1)
            for_t(e, "bK^T")
            for h in range(2):
                half = slice(h * C, (h + 1) * C)
                e.activation(right[half, :, h, :], pairs(ps[4][:, :])[half], ACT.Copy).then_inc(s_ok, 1)
            for_t(e, "Q^T")
            e.activation(QT[:, :, :], pairs(ps[5][:, :]), ACT.Copy).then_inc(s_ok, 1)
            for h in range(2):
                half = slice(h * C, (h + 1) * C)
                e.activation(right[half, :, 2 + h, :], pairs(ps[5][:, :])[half], ACT.Copy).then_inc(s_ok, 1)
            for_g(e, "dd")
            e.activation(DT[:, :, :], dd[:, :, :], ACT.Exp).then_inc(s_ok, 1)

            def group(x, g):
                return x[:, g * GH:(g + 1) * GH, :]

            for g in range(2):
                for_t(e, f"T {g}")
                e.activation(group(T, g), pairs(ps[3 + g][:, :]), ACT.Copy).then_inc(s_ok, 1)
            for lv in range(NL):
                for g in range(2):
                    for_t(e, f"P {lv} {g}")
                    if lv:
                        for_t(e, f"XT {lv - 1} {g}")
                    e.activation(group(P1, g), pairs(ps[(5, 7)[g]][:, :]), ACT.Copy).then_inc(s_ok, 1)
            for_t(e, "KS^T")
            e.activation(KS[:, :, :], pairs(ps[3][:, :]), ACT.Copy).then_inc(s_ok, 1)
            for_t(e, "QS^T")
            e.activation(QS[:, :, :], pairs(ps[4][:, :]), ACT.Copy).then_inc(s_ok, 1)
            for n in range(2):
                for_t(e, f"V {n}")
                x = ps[n][:, :].rearrange("p (a m) -> p a m", a=2)
                y = vn[:, n * W // 2:(n + 1) * W // 2].rearrange("p (a e c) -> p a e c", a=2, e=2)
                for h in range(2):
                    e.activation(y[:, :, h, :], x[:, :, h * (P + C):h * (P + C) + C], ACT.Copy).then_inc(s_ok, 1)
            for_v(e, "O 1 1")
            e.activation(osq[:, :], o[:, :], ACT.Square).then_inc(s_ok, 1)

        @block.vector
        def _(v):
            for n, name in enumerate("qk"):
                for_s(v, f"squares {name}")
                v.tensor_reduce(ssq[:, n * H:(n + 1) * H], heads(sq[:, n, :]), AX.X, ALU.add).then_inc(v_ok, 1)
            for_g(v, "rn")
            v.tensor_tensor(heads(kn[:, :]), heads(ps[1][:, :]), per_row(rn[:, H:]), ALU.mult).then_inc(v_ok, 1)
            v.tensor_tensor(heads(qn[:, :]), heads(ps[0][:, :]), per_row(rn[:, 0:H]), ALU.mult).then_inc(v_ok, 1)
            for_v(v, "kn")
            v.wait_ge(loaded, 16 * LOADS)
            v.tensor_tensor(heads(kb[:, :]), heads(kn[:, :]), per_row(gb[:, H:]), ALU.mult).then_inc(v_ok, 1)
            for_t(v, "rows v")
            v.tensor_tensor(heads(vb[:, :]), heads(ps[2][:, :]), per_row(gb[:, H:]), ALU.mult).then_inc(v_ok, 1)
            v.tensor_tensor(dd[:, :, :], gcB[:, :, :], gb[:, 0:H].unsqueeze(2).to_broadcast([P, H, P]), ALU.subtract)\
                .then_inc(v_ok, 1)
            v.tensor_tensor(td[:, :], g_end[:, :], gb[:, 0:H], ALU.subtract).then_inc(v_ok, 1)
            for_s(v, "eg")
            v.tensor_tensor(bg[:, :], eg[:, :], gb[:, H:], ALU.mult).then_inc(v_ok, 1)
            for_s(v, "D")
            for p, bank in enumerate((0, 1, 2, 6)):
                for_t(v, f"products {p}")
                v.tensor_tensor(NQ[:, p, :, :].rearrange("p (x e) n -> p x e n", x=2),
                                ps[bank][:, :].rearrange("p (x e n) -> p x e n", x=2, e=2),
                                DT[:, 2 * p:2 * p + 2, :].unsqueeze(1).to_broadcast([P, 2, 2, P]), ALU.mult).then_inc(v_ok, 1)
            for_v(v, f"NQ {PAIRS - 1}")
            masked(v, base[:, :, :], M_BASE).then_inc(v_ok, 1)
            for_v(v, "base")
            v.tensor_tensor(TT[:, :, :], base[:, :, :], masks[:, M_EYE:M_EYE + 1, :].to_broadcast([P, H, P]), ALU.add)\
                .then_inc(v_ok, 1)
            for lv in range(NL):
                for kind, x, banks in (("X", T, (0, 1)), ("XT", TT, (2, 6))):
                    for g in range(2):
                        for_t(v, f"{kind} {lv} {g}")
                        if kind == "X":
                            for_t(v, f"XT {lv} {g}")
                        if lv:
                            for_v(v, f"{kind} {lv - 1} {g}")
                        y = x[:, g * GH:(g + 1) * GH, :]
                        v.tensor_tensor(y, y, pairs(ps[banks[g]][:, :]), ALU.subtract).then_inc(v_ok, 1)
            for_t(v, "KS")
            v.tensor_tensor(heads(r1[:, :]), heads(ps[5][:, :]), per_row(bg[:, :]), ALU.mult).then_inc(v_ok, 1)
            for_v(v, "bg KS")
            v.tensor_tensor(r[:, :], vb[:, :], r1[:, :], ALU.subtract).then_inc(v_ok, 1)
            for_s(v, "V 1 1")
            v.tensor_tensor(heads(vg[:, :]), heads(vn[:, :]), per_row(et[:, :]), ALU.mult).then_inc(v_ok, 1)
            for_v(v, "vg")
            for b in range(NS):
                v.tensor_scalar(vgb[:, b, :], vg[:, :], masks[:, M_OWN, b:b + 1], None, ALU.mult).then_inc(v_ok, 1)
            v.wait_ge(states_in, 16 * 2 * PAIRS)
            for e in range(2):
                half = slice(e * C, (e + 1) * C)
                v.tensor_tensor(sgt[half, :, :].rearrange("k (p b) c -> k p b c", p=PAIRS), S[half, :, :, half],
                                gt[half, e::2, :].unsqueeze(3).to_broadcast([C, PAIRS, NS, C]), ALU.mult).then_inc(v_ok, 1)
            for_t(v, "QS")
            v.tensor_tensor(heads(o[:, :]), heads(ps[7][:, :]), per_row(eg[:, :]), ALU.mult).then_inc(v_ok, 1)
            for_v(v, "eg QS")
            for n in range(2):
                for_t(v, f"O {n}")
                x = ps[n][:, :].rearrange("p (a m) -> p a m", a=2)
                y = o[:, n * W // 2:(n + 1) * W // 2].rearrange("p (a e c) -> p a e c", a=2, e=2)
                for h in range(2):
                    z = y[:, :, h, :]
                    v.tensor_tensor(z, z, x[:, :, h * (P + C):h * (P + C) + C], ALU.add).then_inc(v_ok, 1)
            for_s(v, "squares o")
            v.tensor_reduce(oss[:, :], heads(osq[:, :]), AX.X, ALU.add).then_inc(v_ok, 1)
            for n in range(HALVES):
                for_t(v, f"dS {n}")
                p, b = n // 2, n % 2 * HS
                x = ps[(2, 3, 4, 6)[n % 4]][:, :].rearrange("p (b m) -> p b m", b=HS)
                for e in range(2):
                    half = slice(e * C, (e + 1) * C)
                    v.tensor_tensor(S_new[half, p, b:b + HS, :], sgt[half, p * NS + b:p * NS + b + HS, :], x[half, :, half],
                                    ALU.add).then_inc(v_ok, 1)
            for_g(v, "rn o")
            v.tensor_tensor(heads(o[:, :]), heads(o[:, :]), per_row(orn[:, :]), ALU.mult).then_inc(v_ok, 1)
            for_v(v, "on")
            for_g(v, "gate")
            v.tensor_tensor(out[:, :], o[:, :], za[:, :], ALU.mult).then_inc(v_ok, 1)


def rel_table(nc, d, s):
    H, N = s.HB, s.NREL
    with ExitStack() as stack:
        ph = Phase(nc, stack)
        ext = ph.sb("r_ext", [H, s.EXT])
        loaded, filled, stored = ph.sem("r_loaded"), ph.sem("r_filled"), ph.sem("r_stored")
        block = stack.enter_context(nc.Block())

        @block.sync
        def _(sp):
            sp.dma_start(ext[:, 0:N], d.rel).then_inc(loaded, 16)
            sp.wait_ge(filled, 1)
            sp.dma_start(d.rel_ext, ext[:, :]).then_inc(stored, 16)
            sp.wait_ge(stored, 16)

        @block.vector
        def _(v):
            v.wait_ge(loaded, 16)
            v.tensor_copy(ext[:, N:], ext[:, N - 1:N].to_broadcast([H, s.EXT - N])).then_inc(filled, 1)


def reversal(eng, tile, filled):
    eng.memset(tile[:, :], 0.0).then_inc(filled, 1)
    eng.wait_ge(filled, 3)
    eng.affine_select(out=tile[:, :], in_=tile[:, :], compare_op=ALU.not_equal, fill=1.0, base=1 - P,
                      pattern=[[1, P]], channel_multiplier=1).then_inc(filled, 1)


def attend(nc, d, s):
    NT = s.SEQ // P
    H, C = s.HB, s.DB
    PAIRS, W = H // 2, H * C
    BACK = s.BAND // P
    KEYS = s.BAND + P
    NK = BACK + 1
    ROOT = float(C) ** 0.5
    Q0 = W
    assert (NT - BACK - 2) % 2 == 0
    with ExitStack() as stack:
        ph = Phase(nc, stack)
        KT = ph.sb("f_KT", [P, PAIRS, s.SEQ])
        V = ph.sb("f_V", [P, NT, W])
        bias = ph.sb("f_bias", [P, H, KEYS])
        qk = [ph.sb(f"f_qk{i}", [P, 2 * W]) for i in range(2)]
        zb = [ph.sb(f"f_zb{i}", [P, W]) for i in range(2)]
        QT = [ph.sb(f"f_QT{i}", [P, H, P]) for i in range(2)]
        neg = [ph.sb(f"f_neg{i}", [P, KEYS]) for i in range(2)]
        prob = [ph.sb(f"f_prob{i}", [P, KEYS]) for i in range(2)]
        probT = [ph.sb(f"f_probT{i}", [P, NK, P]) for i in range(2)]
        low = [ph.sb(f"f_low{i}", [P, H]) for i in range(2)]
        total = [ph.sb(f"f_total{i}", [P, H]) for i in range(2)]
        inv = [ph.sb(f"f_inv{i}", [P, H]) for i in range(2)]
        o = ph.sb("f_o", [P, W])
        out = [ph.sb(f"f_out{i}", [P, W]) for i in range(2)]
        far = ph.sb("f_far", [P, H])
        ident = ph.sb("f_ident", [P, P])
        anti = ph.sb("f_anti", [P, P])
        near = [prob[i][:, 0:512].rearrange("p (h n) -> p h n", h=4) for i in range(2)]
        near += [probT[i][:, 0:4, :] for i in range(2)]
        score = [ph.ps(f"f_score{i}", [P, 1024]) for i in range(2)]
        turn = ph.ps("f_turn", [P, 1024])
        psO = ph.ps("f_psO", [P, 1024])

        consts, filled, cleared = ph.sem("f_consts"), ph.sem("f_filled"), ph.sem("f_cleared")
        near_ps, bias_ok, masked = ph.sem("f_near_ps"), ph.sem("f_bias_ok"), ph.sem("f_masked")
        qk_in = [ph.sem(f"f_qk_in{i}") for i in range(2)]
        v_in = [ph.sem(f"f_v_in{i}") for i in range(2)]
        z_in = [ph.sem(f"f_z_in{i}") for i in range(2)]
        qkT_ps = ph.sem("f_qkT_ps")
        qT_ok = ph.sem("f_qT_ok")
        kT_ok = ph.sem("f_kT_ok")
        score_ps = ph.sem("f_score_ps")
        neg_ok = ph.sem("f_neg_ok")
        prob_ok = ph.sem("f_prob_ok")
        turn_ps = ph.sem("f_turn_ps")
        probT_ok = ph.sem("f_probT_ok")
        o_ps = ph.sem("f_o_ps")
        inv_ok = ph.sem("f_inv_ok")
        o_ok = ph.sem("f_o_ok")
        out_ok = ph.sem("f_out_ok")
        stored = [ph.sem(f"f_stored{i}") for i in range(2)]
        kv_out = ph.sem("f_kv_out")

        def pipeline(eng, iteration):
            for t in range(BACK):
                iteration(Tile(t, t % 2, t // 2, 2))
            with eng.Fori(0, (NT - BACK - 2) // 2) as i:
                for u in range(2):
                    iteration(Tile(2 * i + (BACK + u), u, i + BACK // 2, 2))
            for t in range(NT - 2, NT):
                iteration(Tile(t, t % 2, t // 2, 2))

        def within(a, ahead):
            return not isinstance(a.t, int) or a.t + ahead < NT

        def keys(a):
            back = min(a.t, BACK) if isinstance(a.t, int) else BACK
            return a.t - back, back + 1

        def slot(a, h):
            if h < H:
                return a, h
            return (a.plus(1), h - H) if within(a, 1) else None

        def heads_before(a, h):
            return H * a.t + h

        block = stack.enter_context(nc.Block())

        @block.sync
        def _(sp):
            with nc.allow_non_contiguous_dma(reason="one bias per head, once"):
                sp.dma_start(far[:, :], d.rel[:, s.NREL - 1].partition_broadcast(P)).then_inc(consts, 16)
            for i in range(4):
                g, first = i % 2, (P + 1, 1)[i // 2]
                near_rows = bass.AP(tensor=d.rel_ext.tensor, offset=g * 4 * s.EXT + first, ap=[[1, P], [s.EXT, 4], [1, P]])
                sp.dma_start(near[i], near_rows).then_inc(consts, 16)

            def load(a):
                at = bass.ds(a.t * P, P)
                sp.dma_start(qk[a.b][:, :], d.rows_b[at, Q0:Q0 + 2 * W]).then_inc(qk_in[a.b], 16)
                sp.dma_start(V[:, a.t, :], d.rows_b[at, Q0 + 2 * W:Q0 + 3 * W]).then_inc(v_in[a.b], 16)

            load(Tile(0, 0, 0, 2))
            load(Tile(1, 1, 0, 2))
            keep = slice(s.SEQ - s.BAND, s.SEQ)
            sp.dma_start(d.k_p, d.rows_b[keep, Q0 + W:Q0 + 2 * W]).then_inc(kv_out, 16)
            sp.dma_start(d.v_p, d.rows_b[keep, Q0 + 2 * W:Q0 + 3 * W]).then_inc(kv_out, 16)

            def store(a):
                sp.wait_ge(out_ok, a.t + 1)
                sp.dma_start(d.mixed[bass.ds(a.t * P, P), W:2 * W], out[a.b][:, :]).then_inc(stored[a.b], 16)

            def iteration(a):
                if within(a, 2):
                    sp.wait_ge(qkT_ps, a.t + 1)
                    sp.wait_ge(o_ps, heads_before(a, 1))
                    load(a.plus(2))
                after_none(sp, out_ok, a.t - 1)
                sp.dma_start(zb[a.b][:, :], d.rows_b[bass.ds(a.t * P, P), Q0 + 3 * W:Q0 + 4 * W]).then_inc(z_in[a.b], 16)
                if not a.first():
                    store(a.prev())

            pipeline(sp, iteration)
            store(Tile(NT - 1, 1, NT // 2 - 1, 2))
            sp.wait_ge(kv_out, 32)
            for b in range(2):
                sp.wait_ge(stored[b], 16 * (1 + NT // 2))

        @block.gpsimd
        def _(g):
            identity(g, ident, filled)
            reversal(g, anti, filled)
            for b in range(2):
                g.memset(QT[b][:, :, :], 0.0).then_inc(cleared, 1)
            g.wait_ge(bias_ok, 5)
            g.wait_ge(cleared, 2)
            g.memset(bias[C:, :, 0:C], -BIG).then_inc(masked, 1)
            g.wait_ge(masked, 1)
            g.memset(bias[0:C, :, KEYS - C:], -BIG).then_inc(masked, 1)

        @block.scalar
        def _(e):
            def probabilities(a, h):
                g = heads_before(a, h)
                e.wait_ge(neg_ok, g + 1)
                after_none(e, turn_ps, g - 1)
                if h == 0:
                    e.wait_ge(inv_ok, 2 * a.t + 2)
                n = keys(a)[1] * P
                e.activation(prob[h % 2][:, 0:n], neg[h % 2][:, 0:n], ACT.Exp, scale=-1.0, bias=low[a.b][:, h:h + 1],
                             accum_out=total[a.b][:, h:h + 1]).then_inc(prob_ok, 1)

            def take_k(a):
                e.wait_ge(qkT_ps, a.t + 1)
                e.activation(KT[:, :, bass.ds(a.t * P, P)], turn[:, 0:PAIRS * P].rearrange("p (a m) -> p a m", a=PAIRS),
                             ACT.Copy).then_inc(kT_ok, 1)

            def transposed(a, h):
                g = heads_before(a, h)
                e.wait_ge(turn_ps, g + 1)
                after_none(e, o_ps, g - 1)
                n = keys(a)[1]
                e.activation(probT[h % 2][:, 0:n, :], turn[:, 0:n * P].rearrange("p (k n) -> p k n", k=n), ACT.Copy)\
                    .then_inc(probT_ok, 1)

            def iteration(a):
                for h in range(H):
                    at = slot(a, h + 1)
                    if at:
                        transposed(*at)
                    at = slot(a, h + 2)
                    if at:
                        probabilities(*at)
                    if h == H // 2 - 2 and within(a, 1):
                        take_k(a.plus(1))

            first = Tile(0, 0, 0, 2)
            take_k(first)
            e.wait_ge(bias_ok, 5)
            probabilities(first, 0)
            transposed(first, 0)
            probabilities(first, 1)
            pipeline(e, iteration)

        @block.tensor
        def _(pe):
            pe.wait_ge(filled, 4)
            pe.wait_ge(consts, 16 * 5)
            for i, bank in enumerate((score[0][:, 0:512], score[1][:, 0:512], turn[:, 0:512], psO[:, 0:512])):
                for h in range(4):
                    last = nc.tensor.matmul(bank[:, h * P:(h + 1) * P], near[i][:, h, :], anti[:, :], start=True, stop=True)
                last.then_inc(near_ps, 1)
            pe.wait_ge(bias_ok, 5)

            def turn_qk(a):
                pe.wait_ge(qk_in[a.b], 16 * (a.n + 1))
                for n, first in ((0, W), (1, 0)):
                    for p in range(PAIRS):
                        last = nc.tensor.transpose(turn[:, (n * PAIRS + p) * P:(n * PAIRS + p + 1) * P],
                                                   qk[a.b][:, first + p * P:first + (p + 1) * P], ident[:, :])
                last.then_inc(qkT_ps, 1)

            def scores(a, h):
                if h == 0:
                    pe.wait_ge(qT_ok, 2 * (a.t + 1))
                    pe.wait_ge(kT_ok, a.t + 1)
                after_none(pe, neg_ok, heads_before(a, h) - 1)
                first, n = keys(a)
                cut = min(n, 4)
                last = nc.tensor.matmul(score[h % 2][:, 0:cut * P], QT[a.b][:, h, :],
                                        KT[:, h // 2, bass.ds(first * P, cut * P)], start=True, stop=True)
                if n > cut:
                    last = nc.tensor.matmul(score[h % 2][:, cut * P:n * P], QT[a.b][:, h, :],
                                            KT[:, h // 2, bass.ds((first + cut) * P, (n - cut) * P)], start=True, stop=True)
                last.then_inc(score_ps, 1)

            def turn_prob(a, h):
                g = heads_before(a, h)
                pe.wait_ge(prob_ok, g + 1)
                after_none(pe, probT_ok, g)
                if h == H // 2 and within(a, 1):
                    pe.wait_ge(qT_ok, 2 * (a.t + 2))
                    pe.wait_ge(kT_ok, a.t + 2)
                for k in range(keys(a)[1]):
                    last = nc.tensor.transpose(turn[:, k * P:(k + 1) * P], prob[h % 2][:, k * P:(k + 1) * P], ident[:, :])
                last.then_inc(turn_ps, 1)

            def values(a, h):
                pe.wait_ge(probT_ok, heads_before(a, h) + 1)
                if h == 0:
                    pe.wait_ge(v_in[a.b], 16 * (a.n + 1))
                if h in (0, H // 2):
                    after_none(pe, o_ok, 4 * a.t - 2 + 4 * h // H)
                first, n = keys(a)
                p = h // 2
                for k in range(n):
                    last = nc.tensor.matmul(psO[:, h * P:(h + 1) * P], probT[h % 2][:, k, :], V[:, first + k, p * P:(p + 1) * P],
                                            start=k == 0, stop=k == n - 1)
                last.then_inc(o_ps, 1)

            def iteration(a):
                for h in range(H):
                    at = slot(a, h + 2)
                    if at:
                        scores(*at)
                    at = slot(a, h + 1)
                    if at:
                        turn_prob(*at)
                    values(a, h)
                    if h == H // 2 - 2 and within(a, 1):
                        pe.wait_ge(probT_ok, heads_before(a, h + 2))
                        turn_qk(a.plus(1))

            first = Tile(0, 0, 0, 2)
            turn_qk(first)
            scores(first, 0)
            scores(first, 1)
            turn_prob(first, 0)
            pipeline(pe, iteration)

        @block.vector
        def _(v):
            v.sem_inc(inv_ok, 4)
            for b in range(2):
                v.sem_inc(stored[b], 16)
            v.wait_ge(consts, 16 * 5)
            v.tensor_scalar(bias[:, :, 0:KEYS - 2 * P], far[:, :].unsqueeze(2).to_broadcast([P, H, KEYS - 2 * P]), ROOT,
                            None, ALU.mult).then_inc(bias_ok, 1)
            for i, bank in enumerate((score[0][:, 0:512], score[1][:, 0:512], turn[:, 0:512], psO[:, 0:512])):
                v.wait_ge(near_ps, i + 1)
                g, k = i % 2, KEYS - 2 * P + i // 2 * P
                v.tensor_scalar(bias[:, g * 4:(g + 1) * 4, k:k + P], bank.rearrange("p (h n) -> p h n", h=4), ROOT, None,
                                ALU.mult).then_inc(bias_ok, 1)

            def take_q(a):
                v.wait_ge(qkT_ps, a.t + 1)
                x = turn[:, :].rearrange("p (n a m) -> p n a m", n=2, a=PAIRS)
                y = QT[a.b][:, :, :].rearrange("p (a e) m -> p a e m", e=2)
                for n in range(2):
                    v.tensor_copy(y[n * C:(n + 1) * C, :, n, :], x[n * C:(n + 1) * C, 1]).then_inc(qT_ok, 1)

            def negated(a, h):
                g = heads_before(a, h)
                waits_apart(v, (bias_ok, 5), [(score_ps, g + 1), (prob_ok, g - 1)])
                n = keys(a)[1] * P
                v.tensor_tensor_reduce(neg[h % 2][:, 0:n], score[h % 2][:, 0:n], bias[:, h, KEYS - n:], -1.0 / ROOT, BIG,
                                       ALU.add, ALU.min, low[a.b][:, h:h + 1]).then_inc(neg_ok, 1)

            def half(a, n):
                v.wait_ge(o_ps, heads_before(a, 4 * n + 4))
                v.reciprocal(inv[a.b][:, 4 * n:4 * n + 4], total[a.b][:, 4 * n:4 * n + 4]).then_inc(inv_ok, 1)
                v.wait_ge(inv_ok, 2 * a.t + n + 5)
                if n == 0:
                    after_none(v, out_ok, a.t)
                x = psO[:, n * 512:(n + 1) * 512].rearrange("p (a m) -> p a m", a=2)
                y = o[:, n * W // 2:(n + 1) * W // 2].rearrange("p (a e c) -> p a e c", a=2, e=2)
                r = inv[a.b][:, 4 * n:4 * n + 4].rearrange("p (a e) -> p a e", e=2)
                for e in range(2):
                    v.tensor_tensor(y[:, :, e, :], x[:, :, e * (P + C):e * (P + C) + C],
                                    r[:, :, e].unsqueeze(2).to_broadcast([P, 2, C]), ALU.mult).then_inc(o_ok, 1)

            def finish(a):
                half(a, 1)
                v.wait_ge(o_ok, 4 * (a.t + 1))
                v.wait_ge(z_in[a.b], 16 * (a.n + 1))
                v.wait_ge(stored[a.b], 16 * (a.n + 1))
                v.tensor_tensor(out[a.b][:, :], o[:, :], zb[a.b][:, :], ALU.mult).then_inc(out_ok, 1)

            def iteration(a):
                for h in range(H):
                    at = slot(a, h + 2)
                    if at:
                        negated(*at)
                    if h == 0 and not a.first():
                        finish(a.prev())
                    if h == H // 2 - 2 and within(a, 1):
                        take_q(a.plus(1))
                    if h == H // 2:
                        half(a, 0)

            v.wait_ge(cleared, 2)
            first = Tile(0, 0, 0, 2)
            take_q(first)
            v.wait_ge(masked, 2)
            v.wait_ge(bias_ok, 5)
            negated(first, 0)
            negated(first, 1)
            pipeline(v, iteration)
            finish(Tile(NT - 1, 1, NT // 2 - 1, 2))


def attend_sample(nc, d, s):
    NS, TS = s.DECB, s.DECT
    H, C = s.HB, s.DB
    PAIRS, W = H // 2, H * C
    KT, KEYS = s.BAND // P, s.BAND + TS
    MAX_REL = (s.NREL - 1) // 2
    ROOT = float(C) ** 0.5
    Q0 = W
    assert H * TS == P and NS % 2 == 0
    with ExitStack() as stack:
        ph = Phase(nc, stack)
        rows = ph.sb("g_rows", [P, 2 * W])
        QT = ph.sb("g_QT", [P, PAIRS, P])
        newT = ph.sb("g_newT", [P, PAIRS, P])
        v_new = ph.sb("g_v_new", [TS, NS, W])
        zb = ph.sb("g_zb", [TS, NS, W])
        out = ph.sb("g_out", [TS, NS, W])
        k = [ph.sb(f"g_k{i}", [P, KT, W]) for i in range(2)]
        v_ = [ph.sb(f"g_v{i}", [P, KT, W]) for i in range(2)]
        STEP = P + 2 * TS
        QB = [ph.sb(f"g_QB{i}", [P, PAIRS * STEP]) for i in range(2)]
        kT = ph.sb("g_kT", [P, PAIRS, KEYS])
        bias = ph.sb("g_bias", [P, KEYS])
        nearA = ph.sb("g_nearA", [P, P])
        nearB = ph.sb("g_nearB", [TS, P])
        neg, prob = ph.sb("g_neg", [P, KEYS]), ph.sb("g_prob", [P, KEYS])
        probT = ph.sb("g_probT", [P, KT, P])
        prob_new = ph.sb("g_prob_new", [TS, P])
        low, total, inv = (ph.sb(f"g_{x}", [P, 1]) for x in ("low", "total", "inv"))
        own = ph.sb("g_own", [P, H])
        own_inv = ph.sb("g_own_inv", [P, H])
        om = ph.sb("g_om", [P, W])
        fold = ph.sb("g_fold", [P, TS])
        ident, anti = ph.sb("g_ident", [P, P]), ph.sb("g_anti", [P, P])
        ps_k = [ph.ps(f"g_ps_k{i}", [P, 512]) for i in range(2)]
        score = ph.ps("g_score", [P, 1024])
        turn = ph.ps("g_turn", [P, 1024])
        psO = ph.ps("g_psO", [P, W])
        psC = ph.ps("g_psC", [P, W])

        consts, filled, cleared = ph.sem("g_consts"), ph.sem("g_filled"), ph.sem("g_cleared")
        start_ps, start_ok = ph.sem("g_start_ps"), ph.sem("g_start_ok")
        k_in = [ph.sem(f"g_k_in{i}") for i in range(2)]
        v_in = [ph.sem(f"g_v_in{i}") for i in range(2)]
        kT_ps = ph.sem("g_kT_ps")
        kT_even, kT_odd = ph.sem("g_kT_even"), ph.sem("g_kT_odd")
        qb_ok = ph.sem("g_qb_ok")
        kn_ok = ph.sem("g_kn_ok")
        score_ps, neg_ok, prob_ok, turn_ps = (ph.sem(f"g_{x}") for x in ("score_ps", "neg_ok", "prob_ok", "turn_ps"))
        probT_ok, new_ok, o_ps, inv_ok = (ph.sem(f"g_{x}") for x in ("probT_ok", "new_ok", "o_ps", "inv_ok"))
        own_ok, om_ok, c_ps, out_ok = (ph.sem(f"g_{x}") for x in ("own_ok", "om_ok", "c_ps", "out_ok"))
        stored = ph.sem("g_stored")
        CONSTS = 16 * 6

        def pipeline(eng, iteration):
            for b in range(2):
                iteration(Tile(b, b, 0, 2))
            with eng.Fori(0, (NS - 4) // 2) as i:
                for u in range(2):
                    iteration(Tile(2 * i + (2 + u), u, i + 1, 2))
            for b in range(NS - 2, NS):
                iteration(Tile(b, b % 2, b // 2, 2))

        def within(a, ahead):
            return not isinstance(a.t, int) or a.t + ahead < NS

        HALF = KEYS // 2

        def halves(x, n):
            return x.rearrange("p (a n) -> p a n", n=n)

        block = stack.enter_context(nc.Block())

        @block.sync
        def _(sp):
            fresh = slice(s.SEQ, s.SEQ + P)

            def by_stream(first):
                return d.rows_b[fresh, first:first + W].rearrange("(b t) c -> t b c", t=TS)

            def load_k(a):
                sp.dma_start(k[a.b][:, :, :], d.cache_k[bass.ds(a.t, 1)].rearrange("o (k p) h c -> p (o k) (h c)", p=P))\
                    .then_inc(k_in[a.b], 16)

            def load_v(a):
                sp.dma_start(v_[a.b][:, :, :], d.cache_v[bass.ds(a.t, 1)].rearrange("o (k p) h c -> p (o k) (h c)", p=P))\
                    .then_inc(v_in[a.b], 16)

            sp.dma_start(rows[:, :], d.rows_b[fresh, Q0:Q0 + 2 * W]).then_inc(consts, 16)
            for tile, count, first in ((nearA, P, MAX_REL - TS + 1), (nearB, TS, MAX_REL - TS + 1 + P)):
                near = bass.AP(tensor=d.rel_ext.tensor, offset=first, ap=[[1, count], [s.EXT, H], [1, TS]])
                sp.dma_start(tile[:, :].rearrange("p (h q) -> p h q", h=H), near).then_inc(consts, 16)
            with nc.allow_non_contiguous_dma(reason="a mask of eight columns, once"):
                sp.dma_start(own[:, :], d.masks[:, M_OWN, 0:H]).then_inc(consts, 16)
            load_k(Tile(0, 0, 0, 2))
            sp.dma_start(v_new[:, :, :], by_stream(Q0 + 2 * W)).then_inc(consts, 16)
            sp.dma_start(zb[:, :, :], by_stream(Q0 + 3 * W)).then_inc(consts, 16)
            load_v(Tile(0, 0, 0, 2))
            load_k(Tile(1, 1, 0, 2))
            load_v(Tile(1, 1, 0, 2))
            sp.dma_start(d.k_s, d.rows_b[fresh, Q0 + W:Q0 + 2 * W]).then_inc(stored, 16)
            sp.dma_start(d.v_s, d.rows_b[fresh, Q0 + 2 * W:Q0 + 3 * W]).then_inc(stored, 16)

            def iteration(a):
                if within(a, 2):
                    sp.wait_ge(kT_ps, PAIRS * (a.t + 1))
                    load_k(a.plus(2))
                    sp.wait_ge(o_ps, a.t + 1)
                    load_v(a.plus(2))

            pipeline(sp, iteration)
            sp.wait_ge(out_ok, NS)
            sp.dma_start(d.mixed[fresh, W:2 * W].rearrange("(b t) c -> t b c", t=TS), out[:, :, :]).then_inc(stored, 16)
            sp.wait_ge(stored, 48)

        @block.gpsimd
        def _(g):
            identity(g, ident, filled)
            reversal(g, anti, filled)
            for b in range(2):
                g.memset(QB[b][:, :], 0.0).then_inc(cleared, 1)

        @block.scalar
        def _(e):
            def front(a):
                for i in range(PAIRS // 2):
                    e.wait_ge(kT_ps, PAIRS * a.t + 2 * i + 1)
                    after_none(e, score_ps, a.t)
                    e.activation(kT[:, 2 * i, 0:s.BAND], ps_k[0][:, :], ACT.Copy).then_inc(kT_even, 1)
                e.wait_ge(neg_ok, a.t + 1)
                after_none(e, turn_ps, a.t)
                after_none(e, inv_ok, a.t)
                e.activation(prob[:, :], neg[:, :], ACT.Exp, scale=-1.0, bias=low[:, :], accum_out=total[:, :])\
                    .then_inc(prob_ok, 1)

            def iteration(a):
                e.wait_ge(turn_ps, a.t + 1)
                after_none(e, o_ps, a.t)
                e.activation(probT[:, :, :], turn[:, 0:KT * P].rearrange("p (k n) -> p k n", k=KT), ACT.Copy)\
                    .then_inc(probT_ok, 1)
                if within(a, 1):
                    front(a.plus(1))

            front(Tile(0, 0, 0, 2))
            pipeline(e, iteration)

        @block.tensor
        def _(pe):
            pe.wait_ge(filled, 4)
            pe.wait_ge(consts, CONSTS)
            for n, bank in ((0, ps_k[0]), (1, ps_k[1])):
                for p in range(PAIRS):
                    at = slice(n * W + p * P, n * W + (p + 1) * P)
                    last = nc.tensor.transpose(bank[:, p * P:(p + 1) * P], rows[:, at], ident[:, :])
                last.then_inc(start_ps, 1)
            nc.tensor.matmul(psO[:, 0:P], nearA[:, :], anti[:, :], start=True, stop=True).then_inc(start_ps, 1)
            nc.tensor.matmul(psO[:, P:P + TS], nearB[:, :], anti[0:TS, P - TS:], start=True, stop=True).then_inc(start_ps, 1)
            pe.wait_ge(start_ok, 6)

            def front(a):
                def keys(p):
                    if p >= 2 or not a.first():
                        done = (PAIRS // 2) * a.t + p // 2
                        pe.wait_ge((kT_even, kT_odd)[p % 2], done)
                    if p == 0:
                        pe.wait_ge(k_in[a.b], 16 * (a.n + 1))
                    for j in range(KT):
                        last = nc.tensor.transpose(ps_k[p % 2][:, j * P:(j + 1) * P], k[a.b][:, j, p * P:(p + 1) * P],
                                                   ident[:, :])
                    last.then_inc(kT_ps, 1)

                def scores(p):
                    pe.wait_ge((kT_even, kT_odd)[p % 2], (PAIRS // 2) * a.t + p // 2 + 1)
                    if p == 0:
                        pe.wait_ge(qb_ok, 2 * (a.t + 1))
                        pe.wait_ge(kn_ok, a.t + 1)
                        after_none(pe, neg_ok, a.t)
                    q, first, last = QB[a.b][:, p * P:(p + 1) * P], p == 0, p == PAIRS - 1
                    for n in range(2):
                        mm = nc.tensor.matmul(halves(score[:, :], 512)[:, n, 0:HALF], q, halves(kT[:, p, :], HALF)[:, n, :],
                                              start=first, stop=last)
                    if last:
                        mm.then_inc(score_ps, 1)

                for p in range(PAIRS):
                    keys(p)
                    if p:
                        scores(p - 1)
                scores(PAIRS - 1)

            def turn_prob(a):
                pe.wait_ge(prob_ok, a.t + 1)
                after_none(pe, probT_ok, a.t)
                after_none(pe, new_ok, a.t)
                for j in range(KT):
                    nc.tensor.transpose(turn[:, j * P:(j + 1) * P], prob[:, j * P:(j + 1) * P], ident[:, :])
                nc.tensor.transpose(turn[0:TS, KT * P:(KT + 1) * P], prob[:, KT * P:], ident[:, :]).then_inc(turn_ps, 1)

            def values(a):
                pe.wait_ge(probT_ok, a.t + 1)
                pe.wait_ge(new_ok, a.t + 1)
                pe.wait_ge(v_in[a.b], 16 * (a.n + 1))
                after_none(pe, om_ok, a.t)
                for j in range(KT):
                    nc.tensor.matmul(psO[:, :], probT[:, j, :], v_[a.b][:, j, :], start=j == 0, stop=False)
                nc.tensor.matmul(psO[:, :], prob_new[:, :], v_new[:, a.t, :], start=False, stop=True).then_inc(o_ps, 1)

            def fold_heads(a):
                pe.wait_ge(om_ok, a.t + 1)
                after_none(pe, out_ok, a.t)
                nc.tensor.matmul(psC[0:TS, :], fold[:, :], om[:, :], start=True, stop=True).then_inc(c_ps, 1)

            def iteration(a):
                turn_prob(a)
                if not a.first():
                    fold_heads(a.prev())
                if within(a, 1):
                    front(a.plus(1))
                values(a)

            front(Tile(0, 0, 0, 2))
            pipeline(pe, iteration)
            fold_heads(Tile(NS - 1, 1, NS // 2 - 1, 2))

        @block.vector
        def _(v):
            v.wait_ge(filled, 4)
            v.tensor_reduce(fold[:, :], ident[:, :].rearrange("p (h q) -> p q h", h=H), AX.X, ALU.add).then_inc(start_ok, 1)
            v.wait_ge(consts, CONSTS)
            for n, x in ((0, QT), (1, newT)):
                v.wait_ge(start_ps, n + 1)
                v.tensor_copy(x[:, :, :], ps_k[n][:, :].rearrange("p (a m) -> p a m", a=PAIRS)).then_inc(start_ok, 1)
            v.wait_ge(start_ps, 4)
            v.tensor_scalar(bias[:, KEYS - P:], psO[:, 0:P], ROOT, None, ALU.mult).then_inc(start_ok, 1)
            v.tensor_scalar(bias[:, KEYS - P - TS:KEYS - P], psO[:, P:P + TS], ROOT, None, ALU.mult).then_inc(start_ok, 1)
            v.wait_ge(start_ok, 5)
            far = KEYS - P - TS
            v.tensor_copy(bias[:, 0:far], bias[:, far:far + 1].to_broadcast([P, far])).then_inc(start_ok, 1)
            v.wait_ge(start_ok, 6)
            v.wait_ge(cleared, 2)

            def front(a):
                after_none(v, score_ps, a.t - 1)
                for e in range(2):
                    half = slice(e * C, (e + 1) * C)
                    x = QB[a.b][half, :].rearrange("p (a n) -> p a n", a=PAIRS)[:, :, e * TS:(e + 1) * TS]
                    v.tensor_copy(x, QT[half, :, bass.ds(a.t * TS, TS)]).then_inc(qb_ok, 1)
                after_none(v, score_ps, a.t)
                v.tensor_copy(kT[:, :, s.BAND:], newT[:, :, bass.ds(a.t * TS, TS)]).then_inc(kn_ok, 1)
                for i in range(PAIRS // 2):
                    v.wait_ge(kT_ps, PAIRS * a.t + 2 * i + 2)
                    v.tensor_copy(kT[:, 2 * i + 1, 0:s.BAND], ps_k[1][:, :]).then_inc(kT_odd, 1)
                waits_apart(v, (start_ok, 6), [(score_ps, a.t + 1), (prob_ok, a.t)])
                v.tensor_tensor_reduce(halves(neg[:, :], HALF), halves(score[:, :], 512)[:, :, 0:HALF], halves(bias[:, :], HALF),
                                       -1.0 / ROOT, BIG, ALU.add, ALU.min, low[:, :])\
                    .then_inc(neg_ok, 1)

            def gate(a):
                v.wait_ge(c_ps, a.t + 1)
                v.tensor_tensor(out[:, a.t, :], psC[0:TS, :], zb[:, a.t, :], ALU.mult).then_inc(out_ok, 1)

            def iteration(a):
                v.wait_ge(prob_ok, a.t + 1)
                v.reciprocal(inv[:, :], total[:, :]).then_inc(inv_ok, 1)
                v.wait_ge(inv_ok, a.t + 1)
                v.tensor_scalar(own_inv[:, :], own[:, :], inv[:, :], None, ALU.mult).then_inc(own_ok, 1)
                v.wait_ge(turn_ps, a.t + 1)
                after_none(v, o_ps, a.t)
                v.tensor_copy(prob_new[:, :], turn[0:TS, KT * P:(KT + 1) * P]).then_inc(new_ok, 1)
                if not a.first():
                    gate(a.prev())
                if within(a, 1):
                    front(a.plus(1))
                v.wait_ge(o_ps, a.t + 1)
                v.wait_ge(own_ok, a.t + 1)
                after_none(v, c_ps, a.t)
                v.tensor_tensor(om[:, :].rearrange("p (h c) -> p h c", h=H), psO[:, :].rearrange("p (h c) -> p h c", h=H),
                                own_inv[:, :].unsqueeze(2).to_broadcast([P, H, C]), ALU.mult).then_inc(om_ok, 1)

            front(Tile(0, 0, 0, 2))
            pipeline(v, iteration)
            gate(Tile(NS - 1, 1, NS // 2 - 1, 2))


def combine(nc, d, s):
    D, KT = s.D, s.D // P
    MIX = 2 * s.HB * s.DB
    MT = MIX // P
    PT = s.PLE // P
    TILES = s.SEQ // P + 1
    BANK = 512
    HALVES = D // BANK
    WEIGHTS = PT + MT + KT
    LOOP = (TILES - 5) // 2
    assert (TILES - 5) % 2 == 0 and MIX == D
    with ExitStack() as stack:
        ph = Phase(nc, stack)
        w_hi = ph.sb("h_w_hi", [P, WEIGHTS, D], F32R)
        w_lo = ph.sb("h_w_lo", [P, WEIGHTS, D], F32R)
        mixed = [ph.sb(f"h_mixed{i}", [P, MIX]) for i in range(2)]
        x = ph.sb("h_x", [P, D])
        p_in_rows = [ph.sb(f"h_p{i}", [P, s.PLE]) for i in range(2)]
        mT_hi = ph.sb("h_mT_hi", [P, MT, P], F32R)
        mT_lo = ph.sb("h_mT_lo", [P, MT, P], F32R)
        hT_hi = ph.sb("h_hT_hi", [P, KT, P], F32R)
        hT_lo = ph.sb("h_hT_lo", [P, KT, P], F32R)
        pT_hi = ph.sb("h_pT_hi", [P, PT, P], F32R)
        pT_lo = ph.sb("h_pT_lo", [P, PT, P], F32R)
        h = [ph.sb(f"h_h{i}", [P, D]) for i in range(2)]
        gain = ph.sb("h_gain", [P, D])
        e = ph.sb("h_e", [P, D])
        sig = ph.sb("h_sig", [P, D])
        y = [ph.sb(f"h_y{i}", [P, D]) for i in range(2)]
        squares = ph.sb("h_squares", [P, D], mybir.dt.bfloat16)
        ssq, var, rstd, exponent = (ph.sb(f"h_{k}", [P, 1]) for k in ("ssq", "var", "rstd", "exponent"))
        ident = ph.sb("h_ident", [P, P])
        psT = ph.ps("h_psT", [P, D])
        psH = ph.ps("h_psH", [P, D])
        psE = ph.ps("h_psE", [P, D])
        psG = ph.ps("h_psG", [P, D])

        consts = ph.sem("h_consts")
        filled = ph.sem("h_filled")
        w_in = [ph.sem(f"h_w_in{k}") for k in range(WEIGHTS)]
        w_hi_ok = ph.sem("h_w_hi_ok")
        w_lo_ok = ph.sem("h_w_lo_ok")
        m_in = [ph.sem(f"h_m_in{i}") for i in range(2)]
        x_in = ph.sem("h_x_in")
        p_in = [ph.sem(f"h_p_in{i}") for i in range(2)]
        mT_ps, m_hi, m_lo = ph.sem("h_mT_ps"), ph.sem("h_m_hi"), ph.sem("h_m_lo")
        hT_ps, h_hi, h_lo = ph.sem("h_hT_ps"), ph.sem("h_h_hi"), ph.sem("h_h_lo")
        pT_ps, p_hi, p_lo = ph.sem("h_pT_ps"), ph.sem("h_p_hi"), ph.sem("h_p_lo")
        h_ps, h_ok = ph.sem("h_h_ps"), ph.sem("h_h_ok")
        e_ps, e_sq, e_var, e_rstd = ph.sem("h_e_ps"), ph.sem("h_e_sq"), ph.sem("h_e_var"), ph.sem("h_e_rstd")
        e_ok = ph.sem("h_e_ok")
        g_ps, sig_ok, ge_ok, y_ok = ph.sem("h_g_ps"), ph.sem("h_sig_ok"), ph.sem("h_ge_ok"), ph.sem("h_y_ok")
        stored = [ph.sem(f"h_stored{i}") for i in range(2)]

        parts_hi, parts_lo = ([w[:, k, :] for k in range(WEIGHTS)] for w in (w_hi, w_lo))
        stages = [y[0][:, :], y[1][:, :], e[:, :], sig[:, :]]

        def weight(k):
            if k < MT:
                return d.w_out[k * P:(k + 1) * P, :]
            if k < PT + MT:
                return d.w_ple[(k - MT) * P:(k - MT + 1) * P, :]
            return d.w_gate[(k - PT - MT) * P:(k - PT - MT + 1) * P, :]

        def half(n):
            return slice(n * BANK, (n + 1) * BANK)

        def pipeline(eng, iteration):
            iteration(Tile(0, 0, 0, 2))
            with eng.Fori(0, LOOP) as i:
                for u in range(2):
                    iteration(Tile(2 * i + (1 + u), (1 + u) % 2, i + (1 + u) // 2, 2))
            for t in range(TILES - 4, TILES):
                iteration(Tile(t, t % 2, t // 2, 2))

        def within(a, ahead):
            return not isinstance(a.t, int) or a.t + ahead < TILES

        def rows(prompt, sample, a):
            if isinstance(a.t, int) and a.t == TILES - 1:
                return sample
            return prompt[bass.ds(a.t * P, P), :]

        block = stack.enter_context(nc.Block())

        @block.sync
        def _(sp):
            sp.dma_start(gain[:, :], d.ple_g.partition_broadcast(P)).then_inc(consts, 16)

            def load_m(a):
                sp.dma_start(mixed[a.b][:, :], d.mixed[bass.ds(a.t * P, P), :]).then_inc(m_in[a.b], 16)

            def load_x(a):
                sp.dma_start(x[:, :], rows(d.x_p, d.x_s, a)).then_inc(x_in, 16)

            def load_p(a):
                sp.dma_start(p_in_rows[a.b][:, :], rows(d.p_p, d.p_s, a)).then_inc(p_in[a.b], 16)

            for t in range(2):
                a = Tile(t, t, 0, 2)
                load_m(a)
                if t == 0:
                    load_x(a)
                load_p(a)
            for k in range(WEIGHTS):
                load_weight(sp, k, stages, weight(k), w_in, w_lo_ok)
                if k == PT + MT:
                    sp.wait_ge(mT_ps, 1)
                    load_m(Tile(2, 0, 1, 2))
            sp.wait_ge(h_ok, HALVES)
            load_x(Tile(1, 1, 0, 2))

            def iteration(a):
                if within(a, 3):
                    sp.wait_ge(mT_ps, a.t + 2)
                    load_m(a.plus(3))
                if within(a, 2):
                    sp.wait_ge(pT_ps, a.t + 1)
                    load_p(a.plus(2))
                    sp.wait_ge(h_ok, HALVES * (a.t + 2))
                    load_x(a.plus(2))
                sp.wait_ge(y_ok, HALVES * (a.t + 1))
                sp.dma_start(rows(d.y_p, d.y_s, a), y[a.b][:, :]).then_inc(stored[a.b], 16)

            pipeline(sp, iteration)
            for b in range(2):
                sp.wait_ge(stored[b], 16 * (1 + (TILES + 1 - b) // 2))

        @block.gpsimd
        def _(g):
            identity(g, ident, filled)
            g.memset(exponent[:, :], -0.5).then_inc(filled, 1)
            g.wait_ge(filled, 3)

            def iteration(a):
                waits_apart(g, (filled, 3), [(e_sq, a.t + 1)])
                g.tensor_scalar(var[:, :], ssq[:, :], 1.0 / D, EPS, ALU.mult, ALU.add).then_inc(e_var, 1)
                g.wait_ge(e_var, a.t + 1)
                g.tensor_tensor(rstd[:, :], var[:, :], exponent[:, :], ALU.pow).then_inc(e_rstd, 1)

            pipeline(g, iteration)

        @block.scalar
        def _(sc):
            def split_weight(k):
                weight_hi(sc, k, stages, parts_hi, w_in, w_hi_ok)

            def split_m(a):
                sc.wait_ge(mT_ps, a.t + 1)
                sc.activation(mT_hi[:, :, :], psT[:, :].rearrange("p (k n) -> p k n", k=MT), ACT.Copy).then_inc(m_hi, 1)

            split_m(Tile(0, 0, 0, 2))
            for k in range(MT):
                split_weight(k)
            split_m(Tile(1, 1, 0, 2))
            for k in range(MT, WEIGHTS):
                split_weight(k)

            def iteration(a):
                sc.wait_ge(hT_ps, a.t + 1)
                sc.activation(hT_hi[:, :, :], psT[:, :].rearrange("p (k n) -> p k n", k=KT), ACT.Copy).then_inc(h_hi, 1)
                sc.wait_ge(pT_ps, a.t + 1)
                sc.activation(pT_hi[:, :, :], psE[:, 0:s.PLE].rearrange("p (k n) -> p k n", k=PT), ACT.Copy).then_inc(p_hi, 1)
                if within(a, 2):
                    split_m(a.plus(2))
                sc.wait_ge(e_ps, a.t + 1)
                if not a.first():
                    sc.wait_ge(e_sq, a.t)
                sc.activation(squares[:, :], psE[:, :], ACT.Square, accum_out=ssq[:, :]).then_inc(e_sq, 1)
                for n in range(HALVES):
                    sc.wait_ge(g_ps, HALVES * a.t + n + 1)
                    if not a.first():
                        sc.wait_ge(ge_ok, HALVES * a.t)
                    sc.activation(sig[:, half(n)], psG[:, half(n)], ACT.Sigmoid).then_inc(sig_ok, 1)

            pipeline(sc, iteration)

        @block.tensor
        def _(pe):
            pe.wait_ge(filled, 2)

            def product(ps, hi, lo, first_k, kt, done, each_half):
                for n in range(HALVES):
                    for k in range(kt):
                        last = matmul3(nc, ps[:, half(n)], hi[:, k, :], lo[:, k, :], w_hi[:, first_k + k, half(n)],
                                       w_lo[:, first_k + k, half(n)], k == 0, k == kt - 1)
                    if each_half or n == HALVES - 1:
                        last.then_inc(done, 1)

            def transpose_m(a):
                pe.wait_ge(m_in[a.b], 16 * (a.n + 1))
                for k in range(MT):
                    last = nc.tensor.transpose(psT[:, k * P:(k + 1) * P], mixed[a.b][:, k * P:(k + 1) * P], ident[:, :])
                last.then_inc(mT_ps, 1)

            def mix(a):
                pe.wait_ge(m_lo, a.t + 1)
                product(psH, mT_hi, mT_lo, 0, MT, h_ps, True)

            transpose_m(Tile(0, 0, 0, 2))
            pe.wait_ge(m_lo, 1)
            for k in range(MT):
                pe.wait_ge(w_lo_ok, k + 1)
                for n in range(HALVES):
                    last = matmul3(nc, psH[:, half(n)], mT_hi[:, k, :], mT_lo[:, k, :], w_hi[:, k, half(n)],
                                   w_lo[:, k, half(n)], k == 0, k == MT - 1)
                    if k == MT - 1:
                        last.then_inc(h_ps, 1)
            transpose_m(Tile(1, 1, 0, 2))

            def iteration(a):
                pe.wait_ge(h_ok, HALVES * (a.t + 1))
                if within(a, 1):
                    pe.wait_ge(m_lo, a.t + 2)
                for k in range(KT):
                    last = nc.tensor.transpose(psT[:, k * P:(k + 1) * P], h[a.b][:, k * P:(k + 1) * P], ident[:, :])
                last.then_inc(hT_ps, 1)
                pe.wait_ge(p_in[a.b], 16 * (a.n + 1))
                pe.wait_ge(e_ok, HALVES * (a.t + 1))
                for k in range(PT):
                    last = nc.tensor.transpose(psE[:, k * P:(k + 1) * P], p_in_rows[a.b][:, k * P:(k + 1) * P], ident[:, :])
                last.then_inc(pT_ps, 1)
                if within(a, 1):
                    mix(a.plus(1))
                pe.wait_ge(h_lo, a.t + 1)
                if within(a, 2):
                    transpose_m(a.plus(2))
                pe.wait_ge(p_lo, a.t + 1)
                if a.first():
                    pe.wait_ge(w_lo_ok, PT + MT)
                product(psE, pT_hi, pT_lo, MT, PT, e_ps, False)
                if a.first():
                    pe.wait_ge(w_lo_ok, WEIGHTS)
                else:
                    pe.wait_ge(sig_ok, HALVES * a.t)
                product(psG, hT_hi, hT_lo, PT + MT, KT, g_ps, True)

            pipeline(pe, iteration)

        @block.vector
        def _(v):
            for b in range(2):
                v.sem_inc(stored[b], 16)
            v.sem_inc(e_ok, HALVES)
            v.wait_ge(consts, 16)

            def split_weight(k):
                weight_lo(v, k, stages, parts_hi, parts_lo, w_hi_ok, w_lo_ok)

            def low(lo, hi, ps, there, done, a):
                v.wait_ge(there, a.t + 1)
                k = lo.shape[1]
                v.tensor_tensor(lo[:, :, :], ps.rearrange("p (k n) -> p k n", k=k), hi[:, :, :].bitcast(F32), ALU.subtract)\
                    .then_inc(done, 1)

            def split_m(a):
                low(mT_lo, mT_hi, psT[:, :], m_hi, m_lo, a)

            def residual(a):
                v.wait_ge(x_in, 16 * (a.t + 1))
                if not (isinstance(a.t, int) and a.t < 2):
                    v.wait_ge(y_ok, HALVES * (a.t - 1))
                for n in range(HALVES):
                    v.wait_ge(h_ps, HALVES * a.t + n + 1)
                    v.tensor_tensor(h[a.b][:, half(n)], psH[:, half(n)], x[:, half(n)], ALU.add).then_inc(h_ok, 1)

            split_m(Tile(0, 0, 0, 2))
            for k in range(MT):
                split_weight(k)
            residual(Tile(0, 0, 0, 2))
            split_m(Tile(1, 1, 0, 2))
            for k in range(MT, WEIGHTS):
                split_weight(k)

            def iteration(a):
                low(hT_lo, hT_hi, psT[:, :], h_hi, h_lo, a)
                low(pT_lo, pT_hi, psE[:, 0:s.PLE], p_hi, p_lo, a)
                if within(a, 1):
                    residual(a.plus(1))
                if within(a, 2):
                    split_m(a.plus(2))
                v.wait_ge(e_rstd, a.t + 1)
                if not a.first():
                    v.wait_ge(y_ok, HALVES * a.t)
                for n in range(HALVES):
                    v.scalar_tensor_tensor(e[:, half(n)], psE[:, half(n)], rstd[:, :], gain[:, half(n)], ALU.mult, ALU.mult)\
                        .then_inc(e_ok, 1)
                for n in range(HALVES):
                    v.wait_ge(sig_ok, HALVES * a.t + n + 1)
                    v.wait_ge(e_ok, HALVES * (a.t + 1) + n + 1)
                    v.tensor_tensor(e[:, half(n)], sig[:, half(n)], e[:, half(n)], ALU.mult).then_inc(ge_ok, 1)
                v.wait_ge(stored[a.b], 16 * (a.n + 1))
                for n in range(HALVES):
                    v.wait_ge(ge_ok, HALVES * a.t + n + 1)
                    v.tensor_tensor(y[a.b][:, half(n)], e[:, half(n)], h[a.b][:, half(n)], ALU.add).then_inc(y_ok, 1)

            pipeline(v, iteration)


class Dram:
    pass


class Sizes:
    pass


def build(nc, args, outs, s, masks):
    d = Dram()
    (x_prompt, x_sample, state_conv, state_gdn, cache_k, cache_v, p_prompt, p_sample, ln_g, w_in, conv_w, a_log,
     dt_bias, gdn_norm_g, q_norm_g, k_norm_g, rel_bias, w_out, w_ple_proj, ple_norm_g, w_ple_gate) = args
    d.x_p, d.x_s = x_prompt[0], x_sample.rearrange("b t c -> (b t) c")
    d.ln_g, d.w_in, d.conv_w, d.a_log, d.dt_bias = ln_g[0], w_in[0], conv_w[0], a_log[0], dt_bias[0]
    d.state_conv, d.state_gdn, d.cache_k, d.cache_v = state_conv[0], state_gdn[0], cache_k[0], cache_v[0]
    d.p_p, d.p_s = p_prompt[0, 0], p_sample[0].rearrange("b t c -> (b t) c")
    d.gdn_g, d.q_g, d.k_g, d.rel = gdn_norm_g[0], q_norm_g[0], k_norm_g[0], rel_bias[0]
    d.w_out, d.w_ple, d.ple_g, d.w_gate = w_out[0], w_ple_proj[0], ple_norm_g[0], w_ple_gate[0]
    (y_p, y_s, conv_p, gdn_p, k_p, v_p, conv_s, gdn_s, k_s, v_s) = outs
    d.y_p, d.y_s = y_p[0], y_s.rearrange("b t c -> (b t) c")
    d.conv_p, d.conv_s = conv_p[0, 0], conv_s[0].rearrange("b t c -> (b t) c")
    d.gdn_p, d.gdn_s = gdn_p[0, 0], gdn_s[0]
    d.k_p, d.v_p = k_p[0, 0].rearrange("t h c -> t (h c)"), v_p[0, 0].rearrange("t h c -> t (h c)")
    d.k_s, d.v_s = k_s[0].rearrange("b t h c -> (b t) (h c)"), v_s[0].rearrange("b t h c -> (b t) (h c)")

    def scratch(name, shape):
        return nc.dram_tensor(name, shape, F32, kind="Internal").ap()

    T = s.SEQ + P
    d.qkvT = scratch("qkvT", [s.QKV, T])
    d.gcT = scratch("gcT", [s.HA, T])
    d.betaT = scratch("betaT", [s.HA, T])
    d.lastT = scratch("lastT", [s.QKV, s.CONVW - 1])
    d.rawT_s = scratch("rawT_s", [s.QKV, P])
    d.mixed = scratch("mixed", [T, 2 * s.HB * s.DB])
    d.masks = masks
    s.EXT = 3 * P
    d.rel_ext = scratch("rel_ext", [s.HB, s.EXT])
    d.rows_b = scratch("rows_b", [T, 5 * s.HB * s.DB])
    project_a(nc, d, s)
    project_b(nc, d, s)
    sample_conv(nc, d, s)
    delta(nc, d, s)
    delta_sample(nc, d, s)
    rel_table(nc, d, s)
    attend(nc, d, s)
    attend_sample(nc, d, s)
    combine(nc, d, s)


def sizes(inputs):
    s = Sizes()
    _, s.SEQ, s.D = inputs["x_prompt"].shape
    s.DECB, s.DECT, _ = inputs["x_sample"].shape
    _, s.CONVW, s.QKV = inputs["conv_w"].shape
    s.HA = inputs["a_log"].shape[1]
    _, s.HB, s.NREL = inputs["rel_bias"].shape
    _, _, s.BAND, _, s.DB = inputs["cache_k"].shape
    s.PLE = inputs["p_prompt"].shape[-1]
    s.DV = inputs["gdn_norm_g"].shape[1]
    return s


INPUTS = ("x_prompt", "x_sample", "state_conv", "state_gdn", "cache_k", "cache_v", "p_prompt", "p_sample", "ln_g", "w_in",
          "conv_w", "a_log", "dt_bias", "gdn_norm_g", "q_norm_g", "k_norm_g", "rel_bias", "w_out", "w_ple_proj",
          "ple_norm_g", "w_ple_gate")


def kernel(**inputs):
    import concourse.bacc as bacc
    from concourse.bass_utils import run_bass_kernel_spmd

    s = sizes(inputs)
    keep = min(s.BAND, s.SEQ)
    outputs = [(1, s.SEQ, s.D), (s.DECB, s.DECT, s.D), (1, 1, s.CONVW - 1, s.QKV), (1, 1, s.HA, s.DV, s.DV),
               (1, 1, keep, s.HB, s.DB), (1, 1, keep, s.HB, s.DB), (1, s.DECB, s.CONVW - 1, s.QKV),
               (1, s.DECB, s.HA, s.DV, s.DV), (1, s.DECB, s.DECT, s.HB, s.DB), (1, s.DECB, s.DECT, s.HB, s.DB)]
    nc = bacc.Bacc("TRN2", target_bir_lowering=False, num_devices=1)
    arrays = {f"in_{name}": np.ascontiguousarray(inputs[name]) for name in INPUTS}
    arrays["in_masks"] = delta_masks(s.DECT)
    args = [nc.dram_tensor(name, a.shape, F32, kind="ExternalInput").ap() for name, a in arrays.items()]
    outs = [nc.dram_tensor(f"out_{i}", shape, F32, kind="ExternalOutput").ap() for i, shape in enumerate(outputs)]
    build(nc, args[:-1], outs, s, args[-1])
    r = run_bass_kernel_spmd(nc, [arrays], core_ids=[0])
    return tuple(r.results[0][f"out_{i}"] for i in range(len(outputs)))
```
